# Optimizing a Trainium2 kernel written in Bass

```python
import math
import jax
import jax.numpy as jnp
from jax import lax
import numpy as np
import jax, jax.numpy as jnp

D_MODEL = 1024
BATCH = 1
SEQ = 512
DEPTH = 1

GLA_HEADS = 4
GLA_DK = 128
GLA_DV = 256
GLA_GATE_RANK = 16
GLA_TAU = 16.0
GLA_CHUNK = 64
NSA_HEADS = 8
NSA_GROUPS = 2
NSA_REP = NSA_HEADS // NSA_GROUPS
NSA_DH = 64
NSA_CMP_LEN = 32
NSA_CMP_STRIDE = 16
NSA_SLC_LEN = 64
NSA_N_SEL = 16
NSA_WINDOW = 512
NSA_Q_BLOCK = 128
D_FF = 2816
RMS_EPS = 1e-6
NEG = -1e30

GLA_QK_W = GLA_HEADS * GLA_DK
GLA_V_W = GLA_HEADS * GLA_DV
NSA_Q_W = NSA_HEADS * NSA_DH
NSA_KV_W = NSA_GROUPS * NSA_DH
NSA_GATE_W = NSA_HEADS * 3
IN_SPLITS = (GLA_QK_W, GLA_QK_W, GLA_V_W, GLA_V_W, GLA_GATE_RANK,
             NSA_Q_W, NSA_KV_W, NSA_KV_W, NSA_KV_W, NSA_KV_W, NSA_KV_W, NSA_KV_W,
             NSA_GATE_W, D_MODEL, D_MODEL)
IN_WIDTH = 4 * GLA_QK_W // 2 + 2 * GLA_V_W + GLA_GATE_RANK + NSA_Q_W + 6 * NSA_KV_W + NSA_GATE_W + 2 * D_MODEL


def rms_norm(x, g):
    xf = x.astype(jnp.float32)
    y = xf * lax.rsqrt(jnp.mean(xf * xf, axis=-1, keepdims=True) + RMS_EPS)
    return (y * g.astype(jnp.float32)).astype(x.dtype)

def masked_softmax(s, mask):
    s = jnp.where(mask, s, NEG)
    p = jax.nn.softmax(s, axis=-1)
    return jnp.where(mask, p, 0.0)

def gla_mixer(q, k, v, r, a_lr, w_alpha2, b_alpha, norm_g):
    B, S = q.shape[0], q.shape[1]
    C = GLA_CHUNK
    nc = S // C

    def heads(t, d):
        return t.reshape(B, nc, C, GLA_HEADS, d).transpose(0, 3, 1, 2, 4).astype(jnp.float32)

    qh = heads(q, GLA_DK) * (GLA_DK ** -0.5)
    kh = heads(k, GLA_DK)
    vh = heads(v, GLA_DV)
    log_a = jax.nn.log_sigmoid((a_lr @ w_alpha2 + b_alpha).astype(jnp.float32)) / GLA_TAU
    b = jnp.cumsum(heads(log_a, GLA_DK), axis=3)
    b_last = b[:, :, :, -1:, :]
    qe = qh * jnp.exp(b)
    ke = kh * jnp.exp(-b)
    kd = kh * jnp.exp(b_last - b)
    causal = jnp.tril(jnp.ones((C, C), dtype=bool))
    attn = jnp.where(causal, jnp.einsum('bhncd,bhnsd->bhncs', qe, ke), 0.0)
    o = jnp.einsum('bhncs,bhnse->bhnce', attn, vh)
    upd = jnp.einsum('bhncd,bhnce->nbhde', kd, vh)
    decay = jnp.exp(b_last[:, :, :, 0, :]).transpose(2, 0, 1, 3)

    def step(state, inp):
        dec, u = inp
        return dec[..., None] * state + u, state

    init = jnp.zeros((B, GLA_HEADS, GLA_DK, GLA_DV), jnp.float32)
    _, s_prev = lax.scan(step, init, (decay, upd))
    o = o + jnp.einsum('bhncd,nbhde->bhnce', qe, s_prev)
    o = o * lax.rsqrt(jnp.mean(o * o, axis=-1, keepdims=True) + RMS_EPS) * norm_g.astype(jnp.float32)
    o = o.reshape(B, GLA_HEADS, S, GLA_DV).transpose(0, 2, 1, 3).reshape(B, S, GLA_V_W)
    return (o * jax.nn.silu(r.astype(jnp.float32))).astype(r.dtype)

def nsa_mixer(q, k_c, v_c, k_s, v_s, k_w, v_w, gate_logits, pe_k, w1_k, w2_k, pe_v, w1_v, w2_v):
    B, S = q.shape[0], q.shape[1]
    G, R, DH = NSA_GROUPS, NSA_REP, NSA_DH
    L, ST, SL, QB, W = NSA_CMP_LEN, NSA_CMP_STRIDE, NSA_SLC_LEN, NSA_Q_BLOCK, NSA_WINDOW
    qh = q.reshape(B, S, G, R, DH).transpose(0, 2, 3, 1, 4).astype(jnp.float32) * (DH ** -0.5)

    def kv_heads(t):
        return t.reshape(B, S, G, DH).transpose(0, 2, 1, 3).astype(jnp.float32)

    gates = jax.nn.sigmoid(gate_logits.astype(jnp.float32)).reshape(B, S, G, R, 3).transpose(0, 2, 3, 1, 4)
    h_idx = jnp.arange(NSA_HEADS, dtype=jnp.float32)
    slopes = jnp.exp2(-8.0 * (h_idx + 1.0) / NSA_HEADS).reshape(1, G, R, 1, 1)

    n_cmp = (S - L) // ST + 1
    starts_c = ST * jnp.arange(n_cmp)
    idx_c = starts_c[:, None] + jnp.arange(L)[None, :]

    def compress(t, pe, w1, w2):
        blocks = t[:, :, idx_c] + pe
        flat = blocks.reshape(B, G, n_cmp, L * DH)
        return jax.nn.silu(flat @ w1) @ w2

    kc = compress(kv_heads(k_c), pe_k, w1_k, w2_k).astype(jnp.float32)
    vc = compress(kv_heads(v_c), pe_v, w1_v, w2_v).astype(jnp.float32)
    end_c = starts_c + L - 1

    n_slc = S // SL
    n_sel = min(NSA_N_SEL, n_slc)
    starts_s = SL * jnp.arange(n_slc)
    ov = jnp.clip(jnp.minimum(starts_c[:, None] + L, starts_s[None, :] + SL)
                  - jnp.maximum(starts_c[:, None], starts_s[None, :]), 0, None).astype(jnp.float32) / L
    ks_blocks = kv_heads(k_s).reshape(B, G, n_slc, SL, DH)
    vs_blocks = kv_heads(v_s).reshape(B, G, n_slc, SL, DH)
    gather = jax.vmap(jax.vmap(lambda blk, ix: blk[ix]))

    kw_pad = jnp.pad(kv_heads(k_w), ((0, 0), (0, 0), (W, 0), (0, 0)))
    vw_pad = jnp.pad(kv_heads(v_w), ((0, 0), (0, 0), (W, 0), (0, 0)))

    nq = S // QB
    q_blocks = qh.reshape(B, G, R, nq, QB, DH).transpose(3, 0, 1, 2, 4, 5)
    g_blocks = gates.reshape(B, G, R, nq, QB, 3).transpose(3, 0, 1, 2, 4, 5)
    jb = jnp.arange(n_slc)
    r_w = jnp.arange(W + QB)

    def attend_block(args):
        i, qb, gb = args
        q0 = i * QB
        t = q0 + jnp.arange(QB)
        tf = t.astype(jnp.float32)
        dist_c = tf[:, None] - end_c[None, :].astype(jnp.float32)
        s_c = jnp.einsum('bgrqd,bgnd->bgrqn', qb, kc) - slopes * dist_c
        p_c = masked_softmax(s_c, end_c[None, :] <= t[:, None])
        o_c = jnp.einsum('bgrqn,bgnd->bgrqd', p_c, vc)
        imp = jnp.einsum('bgrqn,nj->bgqj', p_c, ov)
        cur = t // SL
        forced = (jb[None, :] == 0) | (jb[None, :] == cur[:, None]) | (jb[None, :] == cur[:, None] - 1)
        score = jnp.where(jb[None, :] > cur[:, None], NEG, jnp.where(forced, -NEG, imp))
        _, sel = lax.top_k(score, n_sel)
        ks = gather(ks_blocks, sel).reshape(B, G, QB, n_sel * SL, DH)
        vs = gather(vs_blocks, sel).reshape(B, G, QB, n_sel * SL, DH)
        pos_s = (sel[..., None] * SL + jnp.arange(SL)).reshape(B, G, QB, n_sel * SL)
        dist_s = (tf[None, None, :, None] - pos_s.astype(jnp.float32))[:, :, None]
        s_s = jnp.einsum('bgrqd,bgqkd->bgrqk', qb, ks) - slopes * dist_s
        p_s = masked_softmax(s_s, (pos_s <= t[None, None, :, None])[:, :, None])
        o_s = jnp.einsum('bgrqk,bgqkd->bgrqd', p_s, vs)
        kw = lax.dynamic_slice_in_dim(kw_pad, q0, W + QB, axis=2)
        vw = lax.dynamic_slice_in_dim(vw_pad, q0, W + QB, axis=2)
        pos_w = q0 - W + r_w
        dist_w = t[:, None] - pos_w[None, :]
        mask_w = (pos_w[None, :] >= 0) & (dist_w >= 0) & (dist_w < W)
        s_w = jnp.einsum('bgrqd,bgkd->bgrqk', qb, kw) - slopes * dist_w.astype(jnp.float32)
        p_w = masked_softmax(s_w, mask_w)
        o_w = jnp.einsum('bgrqk,bgkd->bgrqd', p_w, vw)
        return gb[..., 0:1] * o_c + gb[..., 1:2] * o_s + gb[..., 2:3] * o_w

    o = lax.map(attend_block, (jnp.arange(nq), q_blocks, g_blocks))
    return o.transpose(1, 0, 4, 2, 3, 5).reshape(B, S, NSA_Q_W).astype(q.dtype)

def first_inputs(seed: int = 0) -> dict:
    key = jax.random.key(seed)
    ks = jax.random.split(key, 24)
    f32 = jnp.float32

    def normal(k, shape, fan_in):
        return jax.random.normal(k, shape, f32) * (fan_in ** -0.5)

    def gain(k, shape):
        return 1.0 + 0.1 * jax.random.normal(k, shape, f32)

    Ld = DEPTH
    return {
        'x': jax.random.normal(ks[0], (BATCH, SEQ, D_MODEL), f32),
        'norm_mix_pre': gain(ks[1], (Ld, D_MODEL)),
        'norm_mix_post': gain(ks[2], (Ld, D_MODEL)),
        'norm_ffn_pre': gain(ks[3], (Ld, D_MODEL)),
        'norm_ffn_post': gain(ks[4], (Ld, D_MODEL)),
        'w_in': normal(ks[5], (Ld, D_MODEL, IN_WIDTH), D_MODEL),
        'gla_w_alpha2': normal(ks[6], (Ld, GLA_GATE_RANK, GLA_QK_W), GLA_GATE_RANK),
        'gla_b_alpha': 0.1 * jax.random.normal(ks[7], (Ld, GLA_QK_W), f32),
        'gla_norm_g': gain(ks[8], (Ld, GLA_DV)),
        'nsa_cmp_pe_k': 0.1 * jax.random.normal(ks[9], (Ld, NSA_CMP_LEN, NSA_DH), f32),
        'nsa_cmp_w1_k': normal(ks[10], (Ld, NSA_CMP_LEN * NSA_DH, NSA_DH), NSA_CMP_LEN * NSA_DH),
        'nsa_cmp_w2_k': normal(ks[11], (Ld, NSA_DH, NSA_DH), NSA_DH),
        'nsa_cmp_pe_v': 0.1 * jax.random.normal(ks[12], (Ld, NSA_CMP_LEN, NSA_DH), f32),
        'nsa_cmp_w1_v': normal(ks[13], (Ld, NSA_CMP_LEN * NSA_DH, NSA_DH), NSA_CMP_LEN * NSA_DH),
        'nsa_cmp_w2_v': normal(ks[14], (Ld, NSA_DH, NSA_DH), NSA_DH),
        'w_proj_gla': normal(ks[15], (Ld, GLA_V_W, D_MODEL), GLA_V_W),
        'w_proj_nsa': normal(ks[16], (Ld, NSA_Q_W, D_MODEL), NSA_Q_W),
        'w_out': normal(ks[17], (Ld, D_MODEL, D_MODEL), D_MODEL),
        'w_ffn_gate': normal(ks[18], (Ld, D_MODEL, D_FF), D_MODEL),
        'w_ffn_up': normal(ks[19], (Ld, D_MODEL, D_FF), D_MODEL),
        'w_ffn_down': normal(ks[20], (Ld, D_FF, D_MODEL), D_FF),
    }

def first_block(x, norm_mix_pre, norm_mix_post, norm_ffn_pre, norm_ffn_post, w_in,
              gla_w_alpha2, gla_b_alpha, gla_norm_g,
              nsa_cmp_pe_k, nsa_cmp_w1_k, nsa_cmp_w2_k, nsa_cmp_pe_v, nsa_cmp_w1_v, nsa_cmp_w2_v,
              w_proj_gla, w_proj_nsa, w_out, w_ffn_gate, w_ffn_up, w_ffn_down):
    split_points = [int(c) for c in np.cumsum(IN_SPLITS)[:-1]]
    for l in range(DEPTH):
        h = rms_norm(x, norm_mix_pre[l])
        proj = h @ w_in[l]
        (g_q, g_k, g_v, g_r, g_a, n_q, n_kc, n_vc, n_ks, n_vs, n_kw, n_vw,
         n_gate, merge_gla, merge_nsa) = jnp.split(proj, split_points, axis=-1)
        o_gla = gla_mixer(g_q, g_k, g_v, g_r, g_a, gla_w_alpha2[l], gla_b_alpha[l], gla_norm_g[l])
        o_nsa = nsa_mixer(n_q, n_kc, n_vc, n_ks, n_vs, n_kw, n_vw, n_gate,
                          nsa_cmp_pe_k[l], nsa_cmp_w1_k[l], nsa_cmp_w2_k[l],
                          nsa_cmp_pe_v[l], nsa_cmp_w1_v[l], nsa_cmp_w2_v[l])
        mixed = (jax.nn.sigmoid(merge_gla) * (o_gla @ w_proj_gla[l])
                 + jax.nn.sigmoid(merge_nsa) * (o_nsa @ w_proj_nsa[l]))
        x = x + rms_norm(mixed @ w_out[l], norm_mix_post[l])
        h = rms_norm(x, norm_ffn_pre[l])
        f = (jax.nn.silu(h @ w_ffn_gate[l]) * (h @ w_ffn_up[l])) @ w_ffn_down[l]
        x = x + rms_norm(f, norm_ffn_post[l])
    return x


GRID_W = 64
D_MIX = D_MODEL
D_CONV = D_MIX // 2
D_ATTN = D_MIX - D_CONV
HEAD_DIM = 64
N_HEADS = D_ATTN // HEAD_DIM
CONV_WIDTH = 31
NA_ROWS = 8
NA_COLS = 16
D_FF_2 = -(-8 * D_MODEL // (3 * 256)) * 256
D_IN = 2 * D_CONV + 3 * D_ATTN
EPS = 1e-6


def rms_norm_2(x, g):
    xf = x.astype(jnp.float32)
    y = xf * lax.rsqrt(jnp.mean(xf * xf, axis=-1, keepdims=True) + EPS)
    return (y * g.astype(jnp.float32)).astype(x.dtype)

def layer_norm(x, g, b):
    xf = x.astype(jnp.float32)
    mu = jnp.mean(xf, axis=-1, keepdims=True)
    xc = xf - mu
    y = xc * lax.rsqrt(jnp.mean(xc * xc, axis=-1, keepdims=True) + EPS)
    return (y * g.astype(jnp.float32) + b.astype(jnp.float32)).astype(x.dtype)

def conformer_conv(a, gate, dw_kernel, dw_bias, ln_g, ln_b):
    u = a * jax.nn.sigmoid(gate)
    pad = CONV_WIDTH // 2
    y = lax.conv_general_dilated(
        u, dw_kernel[:, None, :], window_strides=(1,), padding=[(pad, pad)],
        dimension_numbers=("NWC", "WIO", "NWC"), feature_group_count=u.shape[-1])
    y = y + dw_bias
    y = layer_norm(y, ln_g, ln_b)
    return jax.nn.silu(y)

def neighbourhood_attention(q, k, v, rpb):
    B, S, H, Dh = q.shape
    rows = S // GRID_W
    kh = min(NA_ROWS, rows)
    kw = NA_COLS
    qg = q.reshape(B, rows, GRID_W, H, Dh)
    kg = k.reshape(B, rows, GRID_W, H, Dh)
    vg = v.reshape(B, rows, GRID_W, H, Dh)
    cols = jnp.arange(GRID_W)
    col_start = jnp.clip(cols - kw // 2, 0, GRID_W - kw)
    col_idx = col_start[:, None] + jnp.arange(kw)[None, :]
    col_bias_idx = col_idx - cols[:, None] + (NA_COLS - 1)
    scale = Dh ** -0.5

    def row_block(r):
        row_start = jnp.clip(r - kh // 2, 0, rows - kh)
        q_r = lax.dynamic_index_in_dim(qg, r, axis=1, keepdims=False)
        k_rows = lax.dynamic_slice_in_dim(kg, row_start, kh, axis=1)
        v_rows = lax.dynamic_slice_in_dim(vg, row_start, kh, axis=1)
        k_win = k_rows[:, :, col_idx]
        v_win = v_rows[:, :, col_idx]
        s = jnp.einsum("bqhd,brqchd->bhqrc", q_r, k_win,
                       preferred_element_type=jnp.float32) * scale
        row_bias_idx = row_start + jnp.arange(kh) - r + (NA_ROWS - 1)
        bias = rpb[:, row_bias_idx][:, :, col_bias_idx]
        s = s + jnp.transpose(bias, (0, 2, 1, 3))[None].astype(jnp.float32)
        p = jax.nn.softmax(s, axis=(-2, -1))
        return jnp.einsum("bhqrc,brqchd->bqhd", p.astype(v_win.dtype), v_win)

    out = lax.map(row_block, jnp.arange(rows))
    return jnp.moveaxis(out, 0, 1).reshape(B, S, H * Dh)

def second_inputs(seed: int = 0) -> dict:
    key = jax.random.key(seed)
    ks = jax.random.split(key, 16)
    f32 = jnp.float32
    n = lambda k, shape, s: (jax.random.normal(k, shape, f32) * s).astype(f32)
    return {
        "x": n(ks[0], (BATCH, SEQ, D_MODEL), 1.0),
        "norm1_g": 1.0 + n(ks[1], (DEPTH, D_MODEL), 0.02),
        "w_in": n(ks[2], (DEPTH, D_MODEL, D_IN), D_MODEL ** -0.5),
        "q_norm_g": 1.0 + n(ks[3], (DEPTH, HEAD_DIM), 0.02),
        "k_norm_g": 1.0 + n(ks[4], (DEPTH, HEAD_DIM), 0.02),
        "rpb": n(ks[5], (DEPTH, N_HEADS, 2 * NA_ROWS - 1, 2 * NA_COLS - 1), 0.1),
        "dw_kernel": n(ks[6], (DEPTH, CONV_WIDTH, D_CONV), CONV_WIDTH ** -0.5),
        "dw_bias": n(ks[7], (DEPTH, D_CONV), 0.02),
        "conv_ln_g": 1.0 + n(ks[8], (DEPTH, D_CONV), 0.02),
        "conv_ln_b": n(ks[9], (DEPTH, D_CONV), 0.02),
        "w_out": n(ks[10], (DEPTH, D_MIX, D_MODEL), D_MIX ** -0.5),
        "norm2_g": 1.0 + n(ks[11], (DEPTH, D_MODEL), 0.02),
        "w_gate": n(ks[12], (DEPTH, D_MODEL, D_FF_2), D_MODEL ** -0.5),
        "w_up": n(ks[13], (DEPTH, D_MODEL, D_FF_2), D_MODEL ** -0.5),
        "w_down": n(ks[14], (DEPTH, D_FF_2, D_MODEL), D_FF_2 ** -0.5),
    }

def second_block(x, norm1_g, w_in, q_norm_g, k_norm_g, rpb, dw_kernel, dw_bias,
              conv_ln_g, conv_ln_b, w_out, norm2_g, w_gate, w_up, w_down):
    B, S, _ = x.shape
    splits = [D_CONV, 2 * D_CONV, 2 * D_CONV + D_ATTN, 2 * D_CONV + 2 * D_ATTN]
    for l in range(DEPTH):
        h = rms_norm_2(x, norm1_g[l])
        z = h @ w_in[l]
        a, gate, q, k, v = jnp.split(z, splits, axis=-1)
        conv_out = conformer_conv(a, gate, dw_kernel[l], dw_bias[l],
                                  conv_ln_g[l], conv_ln_b[l])
        q = rms_norm_2(q.reshape(B, S, N_HEADS, HEAD_DIM), q_norm_g[l])
        k = rms_norm_2(k.reshape(B, S, N_HEADS, HEAD_DIM), k_norm_g[l])
        v = v.reshape(B, S, N_HEADS, HEAD_DIM)
        attn_out = neighbourhood_attention(q, k, v, rpb[l])
        mix = jnp.concatenate([conv_out, attn_out], axis=-1)
        x = x + mix @ w_out[l]
        h = rms_norm_2(x, norm2_g[l])
        x = x + (jax.nn.silu(h @ w_gate[l]) * (h @ w_up[l])) @ w_down[l]
    return x


def setup_inputs(seed=0):
    out = dict(first_inputs(seed))
    for name, value in second_inputs(seed + 1).items():
        if name != "x":
            out[name + "_2"] = value
    return out


def reference(
    x, norm_mix_pre, norm_mix_post, norm_ffn_pre, norm_ffn_post, w_in, gla_w_alpha2,
    gla_b_alpha, gla_norm_g, nsa_cmp_pe_k, nsa_cmp_w1_k, nsa_cmp_w2_k, nsa_cmp_pe_v,
    nsa_cmp_w1_v, nsa_cmp_w2_v, w_proj_gla, w_proj_nsa, w_out, w_ffn_gate, w_ffn_up, w_ffn_down,
    norm1_g_2, w_in_2, q_norm_g_2, k_norm_g_2, rpb_2, dw_kernel_2, dw_bias_2, conv_ln_g_2,
    conv_ln_b_2, w_out_2, norm2_g_2, w_gate_2, w_up_2, w_down_2,
):
    x = first_block(
        x, norm_mix_pre, norm_mix_post, norm_ffn_pre, norm_ffn_post, w_in, gla_w_alpha2,
        gla_b_alpha, gla_norm_g, nsa_cmp_pe_k, nsa_cmp_w1_k, nsa_cmp_w2_k, nsa_cmp_pe_v,
        nsa_cmp_w1_v, nsa_cmp_w2_v, w_proj_gla, w_proj_nsa, w_out, w_ffn_gate, w_ffn_up,
        w_ffn_down,
    )
    return second_block(
        x, norm1_g_2, w_in_2, q_norm_g_2, k_norm_g_2, rpb_2, dw_kernel_2, dw_bias_2,
        conv_ln_g_2, conv_ln_b_2, w_out_2, norm2_g_2, w_gate_2, w_up_2, w_down_2,
    )


_drawn_inputs = setup_inputs


def setup_inputs(seed=0):
    import zlib

    import numpy as np

    out = dict(_drawn_inputs(seed))
    spreads = {}
    factors = {'nsa_cmp_pe_k': 8.0,
     'norm1_g_2': 8.0,
     'q_norm_g_2': 8.0,
     'k_norm_g_2': 8.0,
     'rpb_2': 8.0,
     'dw_bias_2': 20.001,
     'conv_ln_g_2': 29.197,
     'conv_ln_b_2': 31.276,
     'norm2_g_2': 5.865}
    for name, (base, spread) in spreads.items():
        noise = np.random.default_rng([zlib.crc32(name.encode()), seed]).standard_normal(out[name].shape)
        drawn = base * np.exp(spread * noise) if base else spread * noise
        out[name] = jnp.asarray(drawn.astype(out[name].dtype))
    for name, factor in factors.items():
        out[name] = (out[name] * factor).astype(out[name].dtype)
    return out
```

```python
from contextlib import ExitStack

import numpy as np
import concourse.bass as bass
from concourse import mybir

ALU = mybir.AluOpType
ACT = mybir.ActivationFunctionType
F32 = mybir.dt.float32
F32R = mybir.dt.float32r
I32 = mybir.dt.int32
AX = mybir.AxisListType

P = 128
S = 512
TT = S // P
D = 1024
KD = D // P
FF = 2816
KF = FF // P
EPS = 1e-6
NEG = -1e30
GH, DK, DV, RANK, TAU, CH = 4, 128, 256, 16, 16.0, 64
NCH = S // CH
NH, NG, DH = 8, 2, 64
NR = NH // NG
CL, CST = 32, 16
NCMP = (S - CL) // CST + 1
NCP = 32
GATE_ROW = 32
GW, GR, NAC = 64, 8, 16
QC = 16
KC = 32
TAPS = 31
HP = TAPS // 2
BM = 2 * KC - QC
RB_R, RB_C = 2 * GR - 1, 2 * NAC - 1
KEY_BASE = [min(max(QC * i - NAC // 2, 0), GW - KC) for i in range(4)]

GV, GQ, GK, MISC, NQ = 0, 8, 12, 16, 17
KCT, VCT, VST, VWT, KST, KWT, GRR = 21, 22, 23, 24, 25, 26, 27

PHASES = [("in1", GRR, KD), ("r", KD, KD), ("mgn", 2 * KD, KD), ("pg", KD, KD), ("pn", KD, KD // 2),
          ("out1", KD, KD), ("gu1", 2 * KF, KD), ("dn1", KD, KF),
          ("in2", 20, KD), ("out2", KD, KD), ("gu2", 2 * KF, KD), ("dn2", KD, KF)]
CB = 8
CW = CB * P
NBANK = 4


class Phase:
    def __init__(self, name, nt, k, c0, t0, b0):
        self.name, self.nt, self.k, self.c0, self.t0, self.b0 = name, nt, k, c0, t0, b0
        if k == CB // 2:
            self.starts4 = [0, CB]
        else:
            self.starts4 = [n * k + j for n in range(4) for j in range(0, k, CB)]
        self.nc4 = len(self.starts4)
        self.nc = nt * self.nc4 // 4
        self.blocks4 = 4 * k

    def chunk_of(self, tile, k):
        if self.k == CB // 2:
            return tile // 2, (tile % 2) * self.k + k
        return tile * (self.nc4 // 4) + k // CB, k % CB

    def last_chunk(self, tile):
        return self.chunk_of(tile, self.k - 1)[0] + 1


def plan():
    out, c, t, b = {}, 0, 0, 0
    for name, nt, k in PHASES:
        p = Phase(name, nt, k, c, t, b)
        out[name] = p
        c, t, b = c + p.nc, t + nt, b + nt * k
    return out, c, t, b


PH, NCHUNK, NTILE, NBLOCK = plan()

PV_COLS = [("g_mix_pre", KD), ("g_mix_post", KD), ("g_ffn_pre", KD), ("g_ffn_post", KD),
           ("g_norm1", KD), ("g_norm2", KD), ("b_alpha", GH), ("gla_g", DV // P),
           ("dw_bias", 4), ("ln_g", 4), ("ln_b", 4), ("dw", 4 * TAPS), ("qn_g", 1), ("kn_g", 1),
           ("pe_k", CL), ("pe_v", CL)]
PV_AT, _n = {}, 0
for _name, _w in PV_COLS:
    PV_AT[_name] = _n
    _n += _w
NPV = _n
CT_COLS = [("ident", P), ("ones", P), ("pairs", P), ("reset", S), ("causal64", P), ("bias0", S), ("bias1", S),
           ("biasc", TT * NG * NCP), ("maskc", TT * NG * NCP), ("maskn", TT * KC)]
CT_AT, _n = {}, 0
for _name, _w in CT_COLS:
    CT_AT[_name] = (_n, _w)
    _n += _w
NCT = _n


def constants():
    c = np.zeros((P, NCT), np.float32)

    def put(name, a):
        at, w = CT_AT[name]
        c[:, at:at + w] = np.asarray(a, np.float32).reshape(P, w)

    p = np.arange(P)[:, None]
    put("ident", np.eye(P))
    put("ones", np.ones((P, P)))
    put("pairs", p // DH == p.T // DH)
    t = np.arange(S)[None]
    put("reset", np.broadcast_to((t % CH != 0), (P, S)))
    m = np.arange(P)[None]
    put("causal64", (p <= m) & (p // CH == m // CH))
    d = t - (S - P) - p
    dist = np.where(d <= 0, d, NEG)
    for g in range(NG):
        put(f"bias{g}", dist * 2.0 ** -(g * NR + 1))
    n = np.arange(NCP)
    q = np.arange(TT)[None, :, None] * P + p[:, :, None]
    dc = (CST * n + CL - 1)[None, None] - q
    ok = (dc <= 0) & (n < NCMP)[None, None]
    put("biasc", np.stack([np.where(ok, dc, NEG) * 2.0 ** -(g * NR + 1) for g in range(NG)], 2))
    put("maskc", np.stack([ok] * NG, 2))
    cl = np.arange(P) % QC
    mask = np.zeros((P, TT, KC))
    for i in range(TT):
        col = QC * i + cl
        start = np.clip(col - NAC // 2, 0, GW - NAC)
        key = KEY_BASE[i] + np.arange(KC)
        mask[:, i] = np.where((key[None] >= start[:, None]) & (key[None] < start[:, None] + NAC), 0, NEG)
    put("maskn", mask)
    return c


def two_blocks_kernel(nc, A):
    with ExitStack() as ctx:
        def sb(name, shape, dt=F32, scope=ctx):
            return scope.enter_context(nc.sbuf_tensor(name, shape, dt))

        sems = {}

        def sem(name):
            if name not in sems:
                sems[name] = ctx.enter_context(nc.semaphore(name))
            return sems[name]

        xT = sb("xT", [P, KD, S])
        raw = sb("raw", [P, 2, CW])
        wH = sb("wH", [P, 2, CW], F32R)
        wL = sb("wL", [P, 2, CW], F32R)
        aH = sb("aH", [P, KD, S], F32R)
        aL = sb("aL", [P, KD, S], F32R)
        ct = sb("ct", [P, NCT])
        pv = sb("pv", [P, NPV])
        sq = sb("sq", [P, 2, S])
        tmp = sb("tmp", [P, 2, S])
        nx = sb("nx", [P, S])
        nr = sb("nr", [P, S])
        nt_ = sb("nt_", [P, S])
        ssum = sb("ssum", [P, S])

        sc1 = ExitStack()
        pj = sb("pj", [P, 35, S], F32, sc1)
        kcT = sb("kcT", [P, NCP], F32, sc1)
        vcS = sb("vcS", [NG * NCP, P], F32, sc1)
        vsS = sb("vsS", [P, TT, P], F32, sc1)
        vwS = sb("vwS", [P, TT, P], F32, sc1)
        gates = sb("gates", [P, TT, 3 * NH], F32, sc1)
        hid = sb("hid", [P, 2, NCMP], F32, sc1)
        w2k = sb("w2k", [P, DH], F32, sc1)
        w2v = sb("w2v", [P, DH], F32, sc1)
        wa2 = sb("wa2", [RANK, GH * DK], F32, sc1)
        with ExitStack() as early:
            kin_ = sb("kin", [P, 2, CL, NCMP], F32, early)
            w1k = sb("w1k", [P, CL, DH], F32, early)
            w1v = sb("w1v", [P, CL, DH], F32, early)
        kin = [kin_[:, i] for i in range(2)]
        xs = pj[:, 27:35, :].rearrange("p a s -> p (a s)").rearrange("p (t d) -> p t d", t=TT)
        with ExitStack() as gla:
            bT = sb("bT", [P, GH, S], F32, gla)
            qe = sb("qe", [P, S], F32, gla)
            ke = sb("ke", [P, S], F32, gla)
            kd = sb("kd", [P, S], F32, gla)
            kdS = sb("kdS", [P, TT, P], F32, gla)
            vS = sb("vS", [P, TT, DV], F32, gla)
            attnT = sb("attnT", [P, TT, P], F32, gla)
            st = sb("st", [P, NCH - 1, DV], F32, gla)
            dec = sb("dec", [P, NCH], F32, gla)
        with ExitStack() as nsa:
            sb("bT_kept", [P, GH, S], F32, nsa)
            qst = sb("qst", [P, S], F32, nsa)
            sS = sb("sS", [P, 2, S], F32, nsa)
            pS = sb("pS", [P, 2, S], F32, nsa)
            pT = sb("pT", [P, 2, S], F32, nsa)
            scS = sb("scS", [P, TT, NG, NCP], F32, nsa)
            cmx = sb("cmx", [P, TT, NG], F32, nsa)
            nmx = sb("nmx", [P, 2 * NG * TT], F32, nsa)
            rsum = sb("rsum", [P, 3, TT, NG], F32, nsa)
            gsc = sb("gsc", [P, 3, TT, NG], F32, nsa)
            oacc = sb("oacc", [P, TT, P], F32, nsa)
            otmp = sb("otmp", [P, TT, P], F32, nsa)
        with ExitStack() as mrg:
            onH = sb("onH", [P, KD // 2, S], F32R, mrg)
            onL = sb("onL", [P, KD // 2, S], F32R, mrg)
        rs4 = pj[:, KCT:KCT + GH, :]
        sg = pj[:, 0:KD, :]
        sgn = pj[:, KD:2 * KD, :]
        zT = pj[:, KD:2 * KD, :]
        sc1.close()
        with ExitStack() as ffn:
            fH = sb("fH", [P, KF, S], F32R, ffn)
            fL = sb("fL", [P, KF, S], F32R, ffn)
            z2T = sb("z2T", [P, KD, S], F32, ffn)
        with ExitStack() as sc2:
            pk = sb("pk", [P, 20, S], F32, sc2)
            up = sb("up", [P, 4, S + 2 * HP], F32, sc2)
            yT = sb("yT", [P, 4, S], F32, sc2)
            VS = sb("VS", [P, TT, 2, 4 * P], F32, sc2)
            vst = sb("vst", [P, 4, GR * KC], F32, sc2)
            bt = sb("bt", [P, NH, GR, BM], F32, sc2)
            bm = sb("bm", [P, 2, GR, KC], F32, sc2)
            q2 = sb("q2", [P, S], F32, sc2)
            k2 = sb("k2", [P, S], F32, sc2)
            s2 = sb("s2", [P, 2, GR * KC], F32, sc2)
            p2 = sb("p2", [P, 2, GR * KC], F32, sc2)
            pT2 = sb("pT2", [P, 2, GR * KC], F32, sc2)
            nm2 = sb("nm2", [P, 8], F32, sc2)
            rs2 = sb("rs2", [P, 8], F32, sc2)
            o2 = sb("o2", [P, TT, P], F32, sc2)
        with ExitStack() as last:
            os_ = sb("os_", [P, TT, D], F32, last)

        B = [ctx.enter_context(nc.psum_tensor(f"bank{i}", [P, S], F32)) for i in range(8)]

        def cst(name):
            at, w = CT_AT[name]
            return ct[:, at:at + w]

        def vec(name, i=0):
            return pv[:, PV_AT[name] + i:PV_AT[name] + i + 1]

        ident, ones = cst("ident"), cst("ones")
        biasg = [cst("bias0"), cst("bias1")]
        biasc = cst("biasc").rearrange("p (i g n) -> p i g n", g=NG, n=NCP)
        maskc = cst("maskc").rearrange("p (i g n) -> p i g n", g=NG, n=NCP)
        maskn = cst("maskn").rearrange("p (i c) -> p i c", c=KC)
        GROUPS = [(g, br, i) for g in range(NG) for br in range(2) for i in range(TT)]
        NST = len(GROUPS)
        NSQ = NST + 1
        STEPS2 = [(hf, i) for hf in range(2) for i in range(TT)]
        NS2 = len(STEPS2)

        def upd_bank(c):
            half = (c // 2) % 2
            return (B[6], B[7], B[4], B[2])[2 * (c // 4) + c % 2][:, half * DV:(half + 1) * DV]

        R_UNITS = (4, 4, 5, 3)
        M_START, M_STEP, M_END = 3, (2, 2, 1, 1), 5
        M_OUT = (3, 9, 14)
        MBANK = (1, 7)

        block = ctx.enter_context(nc.Block())

        @block.sync
        def _(sp):
            sp.dma_start(xs, A["x"].rearrange("(t p) d -> p t d", p=P)).then_inc(sem("x_landed"), 16)

            def load(c_slot, c_wait, block0):
                if c_wait is not None:
                    sp.wait_ge(sem("w_lo"), c_wait)
                sp.dma_start(raw[:, c_slot, :], A["w"][:, bass.ds(block0 * P, CW)])\
                    .then_inc(sem(f"w_landed{c_slot}"), 16)

            for p in PH.values():
                n4 = p.nt // 4
                if p.c0 == 0:
                    for j in range(4):
                        load(j % 2, j - 1 if j >= 2 else None, p.starts4[j])
                with sp.Fori(1 if p.c0 == 0 else 0, n4) as it:
                    for j in range(p.nc4):
                        load((p.c0 + j) % 2, it * p.nc4 + (p.c0 + j - 1), it * p.blocks4 + (p.b0 + p.starts4[j]))
                for j in range(p.nt % 4):
                    c = n4 * 4 + j
                    load((p.c0 + c) % 2, p.c0 + c - 1, p.b0 + c * CB)
            sp.wait_ge(sem("out_even"), KD // 2)
            sp.wait_ge(sem("out_odd"), KD // 2)
            sp.dma_start(A["out"].rearrange("(t p) d -> p t d", p=P), os_[:]).then_inc(sem("stored"), 16)
            sp.wait_ge(sem("stored"), 16)

        @block.gpsimd
        def _(pool):
            def low(c_slot, n):
                pool.wait_ge(sem("w_hi"), n)
                pool.tensor_tensor(wL[:, c_slot, :], raw[:, c_slot, :], wH[:, c_slot, :].bitcast(F32),
                                   ALU.subtract).then_inc(sem("w_lo"), 1)

            def lows(c0, c1):
                with pool.Fori(0, (c1 - c0) // 2) as it:
                    for j in range(2):
                        low((c0 + j) % 2, it * 2 + (c0 + j + 1))
                if (c1 - c0) % 2:
                    low((c1 - 1) % 2, c1)

            def add_residual(name):
                for kt in range(KD):
                    pool.wait_ge(sem(name + "_mul"), kt + 1)
                    pool.tensor_tensor(xT[:, kt, :], xT[:, kt, :], tmp[:, kt % 2, :], ALU.add).then_inc(sem(name), 1)

            i2 = PH["in2"].c0
            na0 = PH["out2"].c0 + 2
            m = PH["mgn"].c0 + 2
            lows(0, m)
            pool.wait_ge(sem("r_silu"), 1)
            links = 0

            def linked(ins):
                nonlocal links
                links += 1
                ins.then_inc(sem("pool_link"), 1)
                pool.wait_ge(sem("pool_link"), links)

            for h in range(GH):
                pool.wait_ge(sem("gla_rs"), 2)
                rs, t = rs4[:, h, :], nx[:]
                linked(pool.tensor_tensor(t, rs, rs, ALU.mult))
                linked(pool.tensor_tensor(t, t, bT[:, h, :], ALU.mult))
                linked(pool.tensor_scalar(t, t, -0.5, 1.5, ALU.mult, ALU.add))
                linked(pool.tensor_tensor(rs, rs, t, ALU.mult))
                for e in range(2):
                    o = pj[:, GQ + h if e == 0 else GK + h, :]
                    r_ = pj[:, GRR + 2 * h + e, :]
                    linked(pool.tensor_tensor(o, o, rs, ALU.mult))
                    pool.tensor_tensor(r_, o, r_, ALU.mult).then_inc(sem("gla_fin"), 1)
                if h < GH - 1:
                    low((m + h) % 2, m + h + 1)
            pool.wait_ge(sem("gla_fin"), 2 * GH)
            lows(m + GH - 1, PH["gu1"].c0 + 2)
            add_residual("res1")
            lows(PH["gu1"].c0 + 2, i2 + 2)
            add_residual("res2")
            lows(i2 + 2, i2 + 6)
            pool.wait_ge(sem("ffn1_done"), 1)
            pool.memset(bt[:], 0.0).then_inc(sem("bt_zero"), 1)
            pool.memset(up[:], 0.0).then_inc(sem("up_zero"), 1)
            lows(i2 + 6, i2 + 10)
            with pool.Fori(0, 6) as it:
                for j in range(2):
                    low((i2 + j) % 2, it * 2 + (i2 + 10 + j + 1))
                    pool.wait_ge(sem("bank_free"), it * 2 + (NBANK + PH["in2"].t0 + 9 + j))
                    pool.sem_inc(sem("pool_held"), 1)
                    p_ = pk[:, bass.ds(it * 2 + (8 + j), 1), :]
                    pool.tensor_tensor(p_, p_, nr[:].unsqueeze(1), ALU.mult).then_inc(sem("pk_scaled"), 1)
            pool.wait_ge(sem("bt_landed"), 16 * QC)
            with pool.Fori(0, NH // 2) as j:
                for k, (hf, i) in enumerate(STEPS2):
                    off = KEY_BASE[i] - QC * i + NAC
                    pool.wait_ge(sem("na_max"), j * NS2 + (k + 1))
                    pool.sem_inc(sem("pool_held"), 1)
                    pool.tensor_tensor(bm[:, k % 2], bt[:, bass.ds(j * 2 + hf, 1), :, off:off + KC],
                                       maskn[:, i:i + 1, :].to_broadcast([P, GR, KC]), ALU.add)\
                        .then_inc(sem("na_bias"), 1)
            lows(na0, NCHUNK)

        @block.scalar
        def _(act):
            act.dma_start(ct[:], A["ct"]).then_inc(sem("ct_landed"), 16)
            act.dma_start(pv[:], A["pv"]).then_inc(sem("pv_landed"), 16)
            act.dma_start(wa2[:], A["wa2"]).then_inc(sem("small_landed"), 16)
            for name, dst in (("w1k", w1k), ("w1v", w1v)):
                for g in range(NG):
                    act.dma_start(dst[g * DH:(g + 1) * DH], A[name].rearrange("(l d) o -> d l o", d=DH))\
                        .then_inc(sem("small_landed"), 16)
            for name, dst in (("w2k", w2k), ("w2v", w2v)):
                for g in range(NG):
                    act.dma_start(dst[g * DH:(g + 1) * DH], A[name]).then_inc(sem("small_landed"), 16)

            act.preload_act_table_set("natural_log_exp_and_others")

            def high(c_slot, landed, used):
                act.wait_ge(sem(f"w_landed{c_slot}"), landed)
                if used is not None:
                    act.wait_ge(sem("chunk_done"), used)
                act.activation(wH[:, c_slot, :], raw[:, c_slot, :], ACT.Copy).then_inc(sem("w_hi"), 1)

            def ahead(p, j, it=0, last=False):
                if last and p.c0 + p.nc4 * (p.nt // 4 - 1) + j + 2 >= NCHUNK:
                    act.wait_ge(sem("chunk_done"), it * p.nc4 + (p.c0 + j + 1))
                    return
                s = (p.c0 + j) % 2
                n = (p.c0 + j) // 2 + 2
                act.wait_ge(sem(f"w_landed{s}"), it * (p.nc4 * 8) + 16 * n)
                act.wait_ge(sem("chunk_done"), it * p.nc4 + (p.c0 + j + 1))
                act.activation(wH[:, s, :], raw[:, s, :], ACT.Copy).then_inc(sem("w_hi"), 1)

            def ahead_beside(p, j, it, per):
                s = (p.c0 + j) % 2
                act.wait_ge(sem(f"w_landed{s}"), it * (per * 8) + 16 * ((p.c0 + j) // 2 + 2))
                act.wait_ge(sem("chunk_done"), it * per + (p.c0 + j + 1))
                act.activation(wH[:, s, :], raw[:, s, :], ACT.Copy).then_inc(sem("w_hi"), 1)

            def gemm(p, evict=None, mid=None):
                def body(it, tiles, base, last=False, mid=None):
                    q = 0
                    for t in range(tiles):
                        while q < p.last_chunk(t):
                            ahead(p, base * p.nc4 // 4 + q, it, last)
                            q += 1
                        if mid is not None and t == 1:
                            mid()
                        if evict is not None:
                            evict(it, base + t)
                n4 = p.nt // 4
                if mid is not None:
                    body(0, 4, 0, mid=mid)
                    with act.Fori(1, n4) as it:
                        body(it, 4, 0)
                elif p.name == PHASES[-1][0]:
                    with act.Fori(0, n4 - 1) as it:
                        body(it, 4, 0)
                    body(n4 - 1, 4, 0, True)
                else:
                    with act.Fori(0, n4) as it:
                        body(it, 4, 0)
                if p.nt % 4:
                    body(0, p.nt % 4, n4 * 4)

            def square(n, src, it=0, wait=None):
                if wait is not None:
                    act.wait_ge(*wait)
                if n >= 2:
                    act.wait_ge(sem("sq_used"), it * 4 + (n - 1))
                act.activation(sq[:, n % 2, :], src(), ACT.Square).then_inc(sem("sq_ready"), 1)

            def rsqrt(n):
                act.wait_ge(sem("nx_ready"), n)
                act.activation(nr[:], nx[:], ACT.Ln).then_inc(sem("ln_ready"), 1)
                act.wait_ge(sem("ln_ready"), n)
                act.activation(nr[:], nr[:], ACT.Exp, scale=-0.5).then_inc(sem("nr_ready"), 1)

            def high_of_x(use, gain, ready=None, norm=None):
                for kt in range(KD):
                    if ready is not None:
                        act.wait_ge(sem(ready), kt + 1)
                    act.activation(aH[:, kt, :], xT[:, kt, :], ACT.Copy, scale=vec(gain, kt))\
                        .then_inc(sem(use + "_hi"), 1)
                for kt in range(KD if norm is not None else 0):
                    square(norm * KD + kt, lambda: xT[:, kt, :])

            high(0, 16, None)
            high(1, 16, None)
            act.wait_ge(sem("pv_landed"), 16)
            high_of_x("h1", "g_mix_pre", "xT_ready", 0)
            gemm(PH["in1"], mid=lambda: rsqrt(1))

            act.wait_ge(sem("gate_T"), 1)
            act.activation(gates[:], B[6][:].rearrange("p (t c) -> p t c", t=TT)[:, :, GATE_ROW:GATE_ROW + 3 * NH],
                           ACT.Sigmoid).then_inc(sem("gates_ready"), 1)
            act.wait_ge(sem("cmp_hid"), 1)
            for i in range(2):
                act.activation(hid[:, i, :], B[7][:, i * 64:i * 64 + NCMP], ACT.Silu).then_inc(sem("hid_ready"), 1)

            act.preload_act_table_set("natural_log_exp_and_others")
            act.wait_ge(sem("alpha_z"), GH)
            for h in range(GH):
                if h >= 2:
                    act.wait_ge(sem("b_ready"), h - 1)
                lnb = tmp[:, h % 2, :]
                act.activation(lnb, B[h][:], ACT.Abs, bias=vec("b_alpha", h)).then_inc(sem("la_act"), 1)
                act.wait_ge(sem("la_act"), 3 * h + 1)
                act.activation(lnb, lnb, ACT.Exp, scale=-1.0).then_inc(sem("la_act"), 1)
                act.wait_ge(sem("la_act"), 3 * h + 2)
                act.activation(lnb, lnb, ACT.Ln, bias=1.0).then_inc(sem("la_act"), 1)

            act.wait_ge(sem("b_ready"), GH)
            with act.Fori(0, GH) as h:
                bh = bT[:, bass.ds(h, 1), :]
                act.wait_ge(sem("gla_head"), h + 1)
                act.activation(qe[:], bh, ACT.Exp, scale=1 / TAU).then_inc(sem("gla_exp"), 1)
                act.activation(ke[:], bh, ACT.Exp, scale=-1 / TAU).then_inc(sem("gla_exp"), 1)
                act.activation(dec[:], bT[:, bass.ds(h, 1), CH - 1::CH], ACT.Exp, scale=1 / TAU)\
                    .then_inc(sem("gla_exp"), 1)
                act.activation(tmp[:], pj[:, bass.ds(h * 2 + GV, 2), :], ACT.Copy).then_inc(sem("gla_v"), 1)
                act.wait_ge(sem("gla_dif"), h + 1)
                act.activation(kd[:], kd[:], ACT.Exp, scale=1 / TAU).then_inc(sem("gla_exp"), 1)
                act.wait_ge(sem("gla_vT"), h + 1)
                for i in range(2):
                    act.activation(vS[:, 2 * i:2 * i + 2, :], B[i][:].rearrange("p (t e) -> p t e", t=2), ACT.Copy)\
                        .then_inc(sem("gla_vS"), 1)
                act.wait_ge(sem("gla_kdT"), h + 1)
                act.activation(kdS[:], B[4][:].rearrange("p (t e) -> p t e", t=TT), ACT.Copy)\
                    .then_inc(sem("gla_kdS"), 1)
                ahead_beside(PH["r"], 0, h, 2)
                for e in range(2):
                    act.wait_ge(sem("gla_o"), h * 2 + (e + 1))
                    act.activation(sq[:, e, :], B[e][:], ACT.Square).then_inc(sem("gla_sq"), 1)
                ahead_beside(PH["r"], 1, h, 2)
            act.wait_ge(sem("gla_head"), GH + 1)
            act.activation(pj[:, GRR:GRR + KD, :], pj[:, GRR:GRR + KD, :], ACT.Silu).then_inc(sem("r_silu"), 1)
            act.preload_act_table_set("natural_log_exp_and_others")
            act.activation(rs4, bT[:], ACT.Ln).then_inc(sem("gla_rs"), 1)
            act.wait_ge(sem("gla_rs"), 1)
            act.activation(rs4, rs4, ACT.Exp, scale=-0.5).then_inc(sem("gla_rs"), 1)

            with act.Fori(0, NR) as r:
                act.activation(qst[:], pj[:, bass.ds(r + NQ, 1), :], ACT.Copy, scale=DH ** -0.5)\
                    .then_inc(sem("nsa_q"), 1)
                for k, (g, br, i) in enumerate(GROUPS):
                    n = (i + 1) * P
                    act.wait_ge(sem("nsa_max"), r * NST + (k + 3))
                    if k:
                        act.wait_ge(sem("nsa_pT"), r * NSQ + (k + 1))
                    act.activation(pS[:, k % 2, 0:n], sS[:, k % 2, 0:n], ACT.Exp, scale=-1.0, bias=nmx[:, k:k + 1],
                                   accum_out=rsum[:, br, i, g:g + 1]).then_inc(sem("nsa_exp"), 1)
                    if k == 0:
                        act.wait_ge(sem("cmp_sub"), r + 1)
                        act.activation(scS[:], scS[:], ACT.Exp).then_inc(sem("cmp_exp"), 1)
                    if k in M_OUT:
                        ahead_beside(PH["mgn"], M_OUT.index(k), r, 4)
                ahead_beside(PH["mgn"], 3, r, 4)
                act.wait_ge(sem("nsa_oT"), r + 1)
                act.sem_inc(sem("act_held"), 1)
                act.activation(pj[:, bass.ds(r + NQ, 1), :], B[4][:].unsqueeze(1), ACT.Copy).then_inc(sem("nsa_out"), 1)

            act.wait_ge(sem("gla_fin"), 2 * GH)
            for kt in range(KD):
                act.activation(aH[:, kt, :], pj[:, GRR + kt, :], ACT.Copy).then_inc(sem("og_hi"), 1)

            def gate(dst, tiles):
                act.wait_ge(sem("bank_free"), NBANK + PH["mgn"].t0 + tiles)
                act.activation(dst, dst, ACT.Sigmoid).then_inc(sem("gates_mix"), 1)

            gate(sg, KD)

            def gate_and_split():
                gate(sgn, 2 * KD)
                for kt in range(KD // 2):
                    act.activation(onH[:, kt, :], pj[:, NQ + kt, :], ACT.Copy).then_inc(sem("on_hi"), 1)
            gemm(PH["pg"], mid=gate_and_split)

            def high_mix(it, t):
                act.wait_ge(sem("bank_free"), it * 4 + (NBANK + PH["pn"].t0 + t + 1))
                act.activation(aH[:, bass.ds(it * 4 + t, 1), :], sg[:, bass.ds(it * 4 + t, 1), :], ACT.Copy)\
                    .then_inc(sem("mix1_hi"), 1)
            gemm(PH["pn"], high_mix)

            def square_of(p, u, src):
                def after(it, t):
                    square(u * KD + t, lambda: src[:, bass.ds(it * 4 + t, 1), :].rearrange("p o s -> p (o s)"), it,
                           (sem("bank_free"), it * 4 + (NBANK + p.t0 + t + 1)))
                return after

            gemm(PH["out1"], square_of(PH["out1"], 1, zT))
            rsqrt(2)
            high_of_x("h2", "g_ffn_pre", "res1", 2)

            def swiglu(p, tag, norm):
                def silu(it, j):
                    act.wait_ge(sem(tag + "_gate"), it * 2 + (j + 1))
                    act.activation(sq[:, j, :], sq[:, j, :], ACT.Silu).then_inc(sem(tag + "_silu"), 1)

                def high_f(it, j):
                    act.wait_ge(sem(tag + "_f"), it * 2 + (j + 1))
                    act.activation(fH[:, bass.ds(it * 2 + j, 1), :], tmp[:, j, :].unsqueeze(1), ACT.Copy)\
                        .then_inc(sem(tag + "_fH"), 1)
                ahead(p, 0)
                ahead(p, 1)
                rsqrt(norm)
                ahead(p, 2)
                silu(0, 0)
                high_f(0, 0)
                silu(0, 1)
                ahead(p, 3)
                high_f(0, 1)
                with act.Fori(1, p.nt // 4) as it:
                    for j in range(2):
                        ahead(p, 2 * j, it)
                        silu(it, j)
                        ahead(p, 2 * j + 1, it)
                        high_f(it, j)

            swiglu(PH["gu1"], "ff1", 3)
            gemm(PH["dn1"], square_of(PH["dn1"], 3, z2T))
            act.preload_act_table_set("natural_log_exp_and_others")
            rsqrt(4)

            high_of_x("h3", "g_norm1", "res2", 4)

            p = PH["in2"]

            def evict_qkv(it, t):
                act.activation(pk[:, bass.ds(it * 4 + t, 1), :], B[(p.t0 + t) % NBANK][:], ACT.Copy)\
                    .then_inc(sem("bank_free"), 1)

            for t in range(8):
                ahead(p, t)
                if t == 1:
                    rsqrt(5)
            act.wait_ge(sem("bank_free"), NBANK + p.t0 + 8)
            for j in range(4):
                act.activation(pk[:, 4 + j, :], pk[:, 4 + j, :], ACT.Sigmoid).then_inc(sem("glu_sig"), 1)
            act.wait_ge(sem("bt_zero"), 1)
            for c in range(QC):
                act.dma_start(bt[c::QC, :, :, c + 1:c + 1 + RB_C].rearrange("p h r c -> p (h r) c"), A["rpb"])\
                    .then_inc(sem("bt_landed"), 16)
            with act.Fori(2, 5) as it:
                for t in range(4):
                    ahead(p, t, it)
                    evict_qkv(it, t)
            act.preload_act_table_set("natural_log_exp_and_others")
            for j in range(8):
                square(5 * KD + j, lambda: pk[:, 8 + j, :], wait=(sem("pk_scaled"), 12 if j == 0 else j + 1))
                rsqrt(6 + j)
            for j in range(4):
                square(6 * KD + j, lambda: yT[:, j, :], wait=(sem("ln_cen"), j + 1))
            rsqrt(14)
            for j in range(4):
                act.wait_ge(sem("conv_val"), j + 1)
                act.activation(yT[:, j, :], yT[:, j, :], ACT.Silu, scale=vec("ln_g", j), bias=vec("ln_b", j))\
                    .then_inc(sem("conv_silu"), 1)
            for j in range(4):
                act.wait_ge(sem("conv_silu"), j + 1)
                act.activation(aH[:, j, :], yT[:, j, :], ACT.Copy).then_inc(sem("conv_hi"), 1)
            act.preload_act_table_set("natural_log_exp_and_others")
            act.wait_ge(sem("qk_normed"), 8)
            act.wait_ge(sem("pk_scaled"), 12)
            for i in range(TT):
                if i:
                    act.wait_ge(sem("na_VT"), i * 2)
                act.activation(vst[:].rearrange("p j (r c) -> p (j r) c", r=GR),
                               pk[:, 16:20, :].rearrange("p j (r c) -> p (j r) c", r=GR)[:, :, KEY_BASE[i]:KEY_BASE[i] + KC],
                               ACT.Copy).then_inc(sem("na_vst"), 1)
                for hv in range(2):
                    act.wait_ge(sem("na_VT"), i * 2 + hv + 1)
                    act.activation(VS[:, i, hv, :], B[(i * 2 + hv) % 2][:], ACT.Copy).then_inc(sem("na_VS"), 1)
            with act.Fori(0, NH // 2) as j:
                act.wait_ge(sem("na_pair"), j + 1)
                act.activation(q2[:].rearrange("p (i r c) -> p i r c", i=TT, r=GR),
                               pk[:, bass.ds(j + 8, 1), :].rearrange("p o (r i c) -> p (o i) r c", r=GR, i=TT),
                               ACT.Copy, scale=DH ** -0.5).then_inc(sem("na_qk"), 1)
                act.activation(k2[:], pk[:, bass.ds(j + 12, 1), :], ACT.Copy).then_inc(sem("na_qk"), 1)
                for k, (hf, i) in enumerate(STEPS2):
                    act.wait_ge(sem("na_max"), j * NS2 + (k + 3))
                    act.wait_ge(sem("na_pT"), j * NS2 + (k + 1))
                    act.activation(p2[:, k % 2, :], s2[:, k % 2, :], ACT.Exp, scale=-1.0, bias=nm2[:, k:k + 1],
                                   accum_out=rs2[:, k:k + 1]).then_inc(sem("na_exp"), 1)
                act.wait_ge(sem("na_oT"), j + 1)
                act.activation(aH[:, bass.ds(j + 4, 1), :].rearrange("p o (r i c) -> p (o i) r c", r=GR, i=TT),
                               B[7][:].rearrange("p (i r c) -> p i r c", i=TT, r=GR), ACT.Copy)\
                    .then_inc(sem("na_hi"), 1)
            n4 = 6 * KD + 4
            gemm(PH["out2"], lambda it, t: square(n4 + t, lambda: xT[:, bass.ds(it * 4 + t, 1), :].rearrange("p o s -> p (o s)"), it,
                                                  (sem("bank_free"), it * 4 + (NBANK + PH["out2"].t0 + t + 1))))
            high_of_x("h4", "g_norm2")
            swiglu(PH["gu2"], "ff2", 15)
            gemm(PH["dn2"])
            for kt in range(0, KD, 2):
                act.wait_ge(sem("outT"), kt + 1)
                act.activation(os_[:, :, kt * P:(kt + 1) * P], B[4 + kt % 4][:].rearrange("p (t d) -> p t d", t=TT), ACT.Copy)\
                    .then_inc(sem("out_even"), 1)

        @block.tensor
        def _(pe):
            def tile_products(p, it, base, tiles, H, L, first=None, mid=None):
                for t in range(tiles):
                    if mid is not None and t == 2:
                        mid()
                    pe.wait_ge(sem("bank_free"), it * 4 + (p.t0 + base + t + 1))
                    bank = B[(p.t0 + base + t) % NBANK]
                    for k in range(p.k):
                        q, b = p.chunk_of(t, k)
                        q += base * p.nc4 // 4
                        s = (p.c0 + q) % 2
                        if b == 0:
                            pe.wait_ge(sem("w_lo"), it * p.nc4 + (p.c0 + q + 1))
                        if first is not None and t == 0:
                            pe.wait_ge(sem(first), k + 1)
                        hi, lo = wH[:, s, b * P:(b + 1) * P], wL[:, s, b * P:(b + 1) * P]
                        pe.matmul(bank[:], hi, H[:, k, :], start=(k == 0), stop=False)
                        pe.matmul(bank[:], hi, L[:, k, :], start=False, stop=False)
                        mm = pe.matmul(bank[:], lo, H[:, k, :], start=False, stop=(k == p.k - 1))
                        if b == CB - 1 or k == p.k - 1 and p.k != CB // 2:
                            mm.then_inc(sem("chunk_done"), 1)

            def gemm(p, H=aH, L=aL, first=None, mid=None):
                n4 = p.nt // 4
                if first is not None:
                    tile_products(p, 0, 0, 4, H, L, first, mid)
                with pe.Fori(0 if first is None else 1, n4) as it:
                    tile_products(p, it, 0, 4, H, L)
                if p.nt % 4:
                    tile_products(p, 0, n4 * 4, p.nt % 4, H, L)

            def beside(p, it, per, banks, units, ago):
                for u in units:
                    t, k = u // KD, u % KD
                    bank = B[banks[t % len(banks)]]
                    s = (p.c0 + t) % 2
                    if k == 0:
                        pe.wait_ge(sem("bank_free"), it * per + (NBANK + p.t0 + t - ago))
                        pe.wait_ge(sem("w_lo"), it * per + (p.c0 + t + 1))
                    hi, lo = wH[:, s, k * P:(k + 1) * P], wL[:, s, k * P:(k + 1) * P]
                    pe.matmul(bank[:], hi, aH[:, k, :], start=(k == 0), stop=False)
                    pe.matmul(bank[:], hi, aL[:, k, :], start=False, stop=False)
                    mm = pe.matmul(bank[:], lo, aH[:, k, :], start=False, stop=(k == KD - 1))
                    if k == KD - 1:
                        mm.then_inc(sem("chunk_done"), 1)

            def total(used, bank):
                pe.wait_ge(sem("sq_used"), used)
                pe.matmul(bank[:], ones, ssum[:], start=True, stop=True).then_inc(sem("sum_ready"), 1)

            pe.wait_ge(sem("ct_landed"), 16)
            pe.wait_ge(sem("x_landed"), 16)
            for kt in range(KD):
                if kt >= 4:
                    pe.wait_ge(sem("xT_ready"), kt - 3)
                for t in range(TT):
                    mm = pe.transpose(B[4 + kt % 4][:, t * P:(t + 1) * P], xs[:, t, kt * P:(kt + 1) * P], ident)
                mm.then_inc(sem("xT_psum"), 1)
            pe.wait_ge(sem("xT_ready"), KD)
            gemm(PH["in1"], first="h1_lo", mid=lambda: total(KD, B[4]))

            pe.wait_ge(sem("bank_free"), NBANK + PH["r"].t0)
            for tile, bank, name in ((VST, B[4], "v_T"), (VWT, B[5], "v_T"), (MISC, B[6], "gate_T")):
                for t in range(TT):
                    mm = pe.transpose(bank[:, t * P:(t + 1) * P], pj[:, tile, t * P:(t + 1) * P], ident)
                mm.then_inc(sem(name), 1)
            pe.wait_ge(sem("small_landed"), 16 * 9)
            pe.wait_ge(sem("kin_ready"), 4)
            for i, w1 in enumerate((w1k, w1v)):
                for l in range(CL):
                    for g in range(NG):
                        r = slice(g * DH, (g + 1) * DH)
                        mm = pe.matmul(B[7][r, i * 64:i * 64 + NCMP], w1[r, l, :], kin[i][r, l, :],
                                       start=(l == 0), stop=(l == CL - 1))
            mm.then_inc(sem("cmp_hid"), 1)
            for h in range(GH):
                pe.matmul(B[h][:], wa2[:, h * DK:(h + 1) * DK], pj[0:RANK, MISC, :], start=True, stop=True)\
                    .then_inc(sem("alpha_z"), 1)
            pe.wait_ge(sem("hid_ready"), 2)
            pe.wait_ge(sem("v_S"), 2)
            for g in range(NG):
                r = slice(g * DH, (g + 1) * DH)
                pe.matmul(B[4][r, 0:NCMP], w2k[r, :], hid[r, 0, :], start=True, stop=True)
                mm = pe.matmul(B[5 + g][0:NCMP, 0:DH], hid[r, 1, :], w2v[r, :], start=True, stop=True)
            mm.then_inc(sem("cmp_kv"), 1)
            pe.wait_ge(sem("cmp_out"), 1 + NG)
            pe.wait_ge(sem("b_ready"), GH)

            pe.wait_ge(sem("attn_zero"), 1)
            with pe.Fori(0, GH) as h:
                pe.wait_ge(sem("gla_head"), h + 1)
                pe.wait_ge(sem("gla_v"), h + 1)
                for t in range(TT):
                    for e in range(2):
                        mm = pe.transpose(B[t // 2][:, (t % 2) * DV + e * P:(t % 2) * DV + (e + 1) * P],
                                          tmp[:, e, t * P:(t + 1) * P], ident)
                mm.then_inc(sem("gla_vT"), 1)
                at = [0]

                def gate_products():
                    n = R_UNITS[at[0]]
                    first = sum(R_UNITS[:at[0]])
                    beside(PH["r"], h, 2, (3,), range(first, first + n), 0)
                    at[0] += 1
                gate_products()
                pe.wait_ge(sem("gla_qk"), h * 3 + 3)
                for t in range(TT):
                    mm = pe.transpose(B[4][:, t * P:(t + 1) * P], kd[:, t * P:(t + 1) * P], ident)
                mm.then_inc(sem("gla_kdT"), 1)
                for t in range(TT):
                    c = slice(t * P, (t + 1) * P)
                    mm = pe.matmul(B[5][:, c], ke[:, c], qe[:, c], start=True, stop=True)
                mm.then_inc(sem("gla_s"), 1)
                gate_products()
                pe.wait_ge(sem("gla_vS"), h * 2 + 2)
                pe.wait_ge(sem("gla_kdS"), h + 1)
                for c in range(NCH - 1):
                    r = slice((c % 2) * CH, (c % 2) * CH + CH)
                    pe.matmul(upd_bank(c), kdS[r, c // 2, :], vS[r, c // 2, :],
                              start=True, stop=True).then_inc(sem("gla_upd"), 1)
                gate_products()
                pe.wait_ge(sem("gla_att"), h + 1)
                pe.wait_ge(sem("gla_st"), h * (NCH - 1) + (NCH - 1))
                for e in range(2):
                    ec = slice(e * P, (e + 1) * P)
                    for t in range(TT):
                        pe.matmul(B[e][:, t * P:(t + 1) * P], vS[:, t, ec], attnT[:, t, :], start=True, stop=(t == 0),
                                  skip_group_check=True)
                        for c in (2 * t, 2 * t + 1):
                            if c:
                                cc = slice(c * CH, (c + 1) * CH)
                                mm = pe.matmul(B[e][:, cc], st[:, c - 1, ec], qe[:, cc], start=False, stop=True,
                                               skip_group_check=True)
                    mm.then_inc(sem("gla_o"), 1)
                gate_products()
                pe.wait_ge(sem("gla_sq"), h * 2 + 2)
                pe.matmul(B[4][:], ones, sq[:, 0, :], start=True, stop=False)
                pe.matmul(B[4][:], ones, sq[:, 1, :], start=False, stop=True).then_inc(sem("gla_ms"), 1)

            pe.wait_ge(sem("gla_head"), GH + 1)
            kT = (pj[:, KST, :], pj[:, KWT, :])
            vv = (vsS, vwS)
            with pe.Fori(0, NR) as r:
                done = [0]

                def gate_products(n):
                    beside(PH["mgn"], r, 4, MBANK, range(done[0], done[0] + n), 1)
                    done[0] += n
                gate_products(M_START)
                pe.wait_ge(sem("nsa_q"), r + 1)
                pe.wait_ge(sem("nsa_max"), r * NST + 2)
                for g in range(NG):
                    row = slice(g * DH, (g + 1) * DH)
                    for i in range(TT):
                        mm = pe.matmul(B[2 + g][:, i * NCP:(i + 1) * NCP], qst[row, i * P:(i + 1) * P], kcT[row, :],
                                       start=True, stop=True)
                    mm.then_inc(sem("cmp_s"), 1)
                for k in range(NSQ + 2):
                    if k < NST:
                        g, br, i = GROUPS[k]
                        row = slice(g * DH, (g + 1) * DH)
                        if k < NG:
                            pe.wait_ge(sem("cmp_read"), r * NG + k + 1)
                        else:
                            pe.wait_ge(sem("nsa_max"), r * NST + (k + 1))
                        pe.matmul(B[2 + k % 2][:, 0:(i + 1) * P], qst[row, i * P:(i + 1) * P],
                                  kT[br][row, 0:(i + 1) * P], start=True, stop=True).then_inc(sem("nsa_s"), 1)
                        gate_products(M_STEP[i])
                    if 1 <= k <= NST:
                        q = k - 1
                        g, br, i = GROUPS[q]
                        pe.wait_ge(sem("nsa_exp"), r * NST + (q + 1))
                        pe.wait_ge(sem("nsa_pTS"), r * NSQ + (2 if q == 0 else q + 1))
                        for kt in range(i + 1):
                            mm = pe.transpose(B[4 * (q % 2)][:, kt * P:(kt + 1) * P], pS[:, q % 2, kt * P:(kt + 1) * P],
                                              ident)
                        mm.then_inc(sem("nsa_pT"), 1)
                    if k == NSQ:
                        pe.wait_ge(sem("cmp_p"), r + 1)
                        pe.wait_ge(sem("nsa_pTS"), r * NSQ + NSQ)
                        pe.sem_inc(sem("pe_held"), 1)
                        for i in range(TT):
                            mm = pe.transpose(B[0][0:NG * NCP, i * P:(i + 1) * P],
                                              scS[:, i, :, :].rearrange("p g n -> p (g n)"), ident)
                        mm.then_inc(sem("nsa_pT"), 1)
                    if 2 <= k <= NST + 1:
                        q = k - 2
                        g, br, i = GROUPS[q]
                        pe.wait_ge(sem("nsa_pTS"), r * NSQ + (q + 3))
                        for kt in range(i + 1):
                            mm = pe.matmul(B[5 + br][:, i * P + g * DH:i * P + (g + 1) * DH],
                                           pT[:, q % 2, kt * P:(kt + 1) * P], vv[br][:, kt, g * DH:(g + 1) * DH],
                                           start=(kt == 0), stop=(kt == i))
                        mm.then_inc(sem("nsa_pv"), 1)
                pe.wait_ge(sem("nsa_pTS"), r * NSQ + (NST + 3))
                for i in range(TT):
                    mm = pe.matmul(B[3][:, i * P:(i + 1) * P], pT[0:NG * NCP, 0, i * P:(i + 1) * P], vcS[:],
                                   start=True, stop=True)
                mm.then_inc(sem("nsa_pv"), 1)
                gate_products(M_END)
                pe.wait_ge(sem("nsa_acc"), r + 1)
                for i in range(TT):
                    mm = pe.transpose(B[4][:, i * P:(i + 1) * P], oacc[:, i, :], ident)
                mm.then_inc(sem("nsa_oT"), 1)

            pe.wait_ge(sem("nsa_out"), NR)
            pe.wait_ge(sem("bank_free"), NBANK + PH["pg"].t0)
            gemm(PH["pg"], first="og_lo")
            pe.wait_ge(sem("on_lo"), KD // 2)
            gemm(PH["pn"], onH, onL)
            gemm(PH["out1"], first="mix1_lo")
            total(2 * KD, B[4])
            gemm(PH["gu1"], first="h2_lo", mid=lambda: total(3 * KD, B[5]))
            pe.wait_ge(sem("ff1_fL"), KF + 2)
            gemm(PH["dn1"], fH, fL)
            total(4 * KD, B[4])
            gemm(PH["in2"], first="h3_lo", mid=lambda: total(5 * KD, B[5]))
            for j in range(8):
                pe.wait_ge(sem("sq_ready"), 8 * 5 + j + 1)
                if j >= 2:
                    pe.wait_ge(sem("nx_ready"), 5 + j - 1)
                pe.matmul(B[4 + j % 2][:], cst("pairs"), sq[:, j % 2, :], start=True, stop=True)\
                    .then_inc(sem("sq_used"), 1)
            pe.wait_ge(sem("conv_done"), 4)
            for j in range(4):
                mm = pe.matmul(B[6][:], ones, yT[:, j, :], start=(j == 0), stop=(j == 3))
            mm.then_inc(sem("ln_sum"), 1)
            for j in range(4):
                pe.wait_ge(sem("sq_ready"), 8 * 6 + j + 1)
                pe.matmul(B[7][:], ones, sq[:, j % 2, :], start=(j == 0), stop=(j == 3)).then_inc(sem("sq_used"), 1)
            pe.wait_ge(sem("bank_free"), NBANK + PH["out2"].t0)
            for i in range(TT):
                for hv in range(2):
                    n = i * 2 + hv
                    if n >= 2:
                        pe.wait_ge(sem("na_VS"), n - 1)
                    pe.wait_ge(sem("na_vst"), i + 1)
                    for j in range(4):
                        mm = pe.transpose(B[n % 2][:, j * P:(j + 1) * P], vst[:, j, hv * P:(hv + 1) * P], ident)
                    mm.then_inc(sem("na_VT"), 1)
            pe.wait_ge(sem("na_VS"), 8)
            kg = k2[:].rearrange("p (r c) -> p r c", r=GR)
            with pe.Fori(0, NH // 2) as j:
                pe.wait_ge(sem("na_qk"), j * 2 + 2)
                for k in range(NS2 + 2):
                    if k < NS2:
                        hf, i = STEPS2[k]
                        row = slice(hf * DH, (hf + 1) * DH)
                        pe.wait_ge(sem("na_max"), j * NS2 + (k + 1))
                        pe.matmul(B[2 + k % 2][:, 0:GR * KC], q2[row, i * P:(i + 1) * P],
                                  kg[row, :, KEY_BASE[i]:KEY_BASE[i] + KC], start=True, stop=True)\
                            .then_inc(sem("na_s"), 1)
                    if 1 <= k <= NS2:
                        q = k - 1
                        pe.wait_ge(sem("na_exp"), j * NS2 + (q + 1))
                        pe.wait_ge(sem("na_pTS"), j * NS2 + (q + 1))
                        for hv in range(2):
                            mm = pe.transpose(B[4 + q % 2][:, hv * P:(hv + 1) * P], p2[:, q % 2, hv * P:(hv + 1) * P],
                                              ident)
                        mm.then_inc(sem("na_pT"), 1)
                    if k >= 2:
                        q = k - 2
                        hf, i = STEPS2[q]
                        pe.wait_ge(sem("na_pTS"), j * NS2 + (q + 3))
                        for hv in range(2):
                            mm = pe.matmul(B[6][:, i * P + hf * DH:i * P + (hf + 1) * DH], pT2[:, q % 2, hv * P:(hv + 1) * P],
                                           VS[:, i, hv, bass.ds(j * P + hf * DH, DH)], start=(hv == 0), stop=(hv == 1))
                        mm.then_inc(sem("na_pv"), 1)
                pe.wait_ge(sem("na_norm"), j + 1)
                for i in range(TT):
                    mm = pe.transpose(B[7][:, i * P:(i + 1) * P], o2[:, i, :], ident)
                mm.then_inc(sem("na_oT"), 1)
            pe.wait_ge(sem("conv_lo"), 4)
            pe.wait_ge(sem("na_pair"), NH // 2 + 1)
            gemm(PH["out2"])
            gemm(PH["gu2"], first="h4_lo", mid=lambda: total(7 * KD + 4, B[4]))
            pe.wait_ge(sem("ff2_fL"), KF + 2)
            gemm(PH["dn2"], fH, fL)
            for kt in range(KD):
                pe.wait_ge(sem("bank_free"), NBANK + PH["dn2"].t0 + kt + 1)
                if kt >= 4:
                    pe.wait_ge(sem("out_odd" if kt % 2 else "out_even"), kt // 2 - 1)
                for t in range(TT):
                    mm = pe.transpose(B[4 + kt % 4][:, t * P:(t + 1) * P], xT[:, kt, t * P:(t + 1) * P], ident)
                mm.then_inc(sem("outT"), 1)

        @block.vector
        def _(dve):
            chain = [0]

            def link(ins):
                chain[0] += 1
                ins.then_inc(sem("dve_link"), 1)
                dve.wait_ge(sem("dve_link"), chain[0])

            dve.memset(nr[:, 0:1], 0.0).then_inc(sem("bank_free"), NBANK)
            for name, n in (("gla_head", 1), ("nsa_max", 2), ("nsa_pT", 2), ("nsa_pTS", 2),
                            ("na_max", 2), ("na_pT", 2), ("na_pTS", 2), ("na_pair", 1), ("ff1_fL", 2), ("ff2_fL", 2)):
                dve.sem_inc(sem(name), n)

            def newton(n):
                dve.wait_ge(sem("nr_ready"), n)
                link(dve.scalar_tensor_tensor(nt_[:], nr[:], -0.5, nr[:], ALU.mult, ALU.mult))
                link(dve.tensor_tensor(nt_[:], nt_[:], nx[:], ALU.mult))
                link(dve.scalar_tensor_tensor(nr[:], nt_[:], 1.5, nr[:], ALU.add, ALU.mult))

            def clear_sum(n):
                if n:
                    dve.wait_ge(sem("sum_ready"), n)
                link(dve.memset(ssum[:], 0.0))

            def add_square(n, it=0):
                dve.wait_ge(sem("sq_ready"), it * 4 + (n + 1))
                dve.wait_ge(sem("sq_used"), it * 4 + n)
                dve.tensor_tensor(ssum[:], ssum[:], sq[:, n % 2, :], ALU.add).then_inc(sem("sq_used"), 1)

            def norm(sums, n, bank):
                dve.wait_ge(sem("sum_ready"), sums)
                dve.tensor_scalar(nx[:], bank[:], 1.0 / D, EPS, ALU.mult, ALU.add).then_inc(sem("nx_ready"), 1)
                newton(n)

            def low_of_x(use, gain, kt):
                dve.wait_ge(sem(use + "_hi"), kt + 1)
                dve.scalar_tensor_tensor(aL[:, kt, :], xT[:, kt, :], vec(gain, kt), aH[:, kt, :].bitcast(F32),
                                         ALU.mult, ALU.subtract).then_inc(sem(use + "_lo"), 1)

            def low_of(use, src, n):
                for kt in range(n):
                    dve.wait_ge(sem(use + "_hi"), kt + 1)
                    dve.tensor_tensor(aL[:, kt, :], src(kt), aH[:, kt, :].bitcast(F32), ALU.subtract)\
                        .then_inc(sem(use + "_lo"), 1)

            def evict(p, write, groups=None):
                def body(it, base, tiles):
                    for t in range(tiles):
                        dve.wait_ge(sem("chunk_done"), it * p.nc4 + (p.c0 + base * p.nc4 // 4 + p.last_chunk(t)))
                        write(it, base + t, B[(p.t0 + base + t) % NBANK])
                n4 = p.nt // 4 if groups is None else groups
                with dve.Fori(0, n4) as it:
                    body(it, 0, 4)
                if groups is None and p.nt % 4:
                    body(0, n4 * 4, p.nt % 4)

            def normed_to(dst):
                def write(it, t, bank):
                    dve.tensor_tensor(dst[:, bass.ds(it * 4 + t, 1), :], bank[:].unsqueeze(1), nr[:].unsqueeze(1), ALU.mult)\
                        .then_inc(sem("bank_free"), 1)
                return write

            def copy_and_square(dst, u):
                def write(it, t, bank):
                    dve.tensor_scalar(dst[:, bass.ds(it * 4 + t, 1), :], bank[:], 1.0, None, ALU.mult).then_inc(sem("bank_free"), 1)
                    add_square(u * KD + t, it)
                return write

            dve.wait_ge(sem("pv_landed"), 16)
            for kt in range(KD):
                dve.wait_ge(sem("xT_psum"), kt + 1)
                dve.tensor_copy(xT[:, kt, :], B[4 + kt % 4][:]).then_inc(sem("xT_ready"), 1)
                if kt:
                    low_of_x("h1", "g_mix_pre", kt - 1)
            low_of_x("h1", "g_mix_pre", KD - 1)
            clear_sum(0)
            for kt in range(KD):
                add_square(kt)
            norm(1, 1, B[4])
            evict(PH["in1"], normed_to(pj))

            dve.wait_ge(sem("bank_free"), NBANK + PH["r"].t0)
            for i, (tile, pe_name) in enumerate(((KCT, "pe_k"), (VCT, "pe_v"))):
                for a in range(CL // CST):
                    src = pj[:, tile, a * CST:a * CST + NCMP * CST].rearrange("p (n b) -> p b n", b=CST)
                    pos = pv[:, PV_AT[pe_name] + a * CST:PV_AT[pe_name] + (a + 1) * CST].unsqueeze(2)\
                        .to_broadcast([P, CST, NCMP])
                    dve.tensor_tensor(kin[i][:, a * CST:(a + 1) * CST, :], src, pos, ALU.add).then_inc(sem("kin_ready"), 1)
            dve.wait_ge(sem("v_T"), 2)
            dve.tensor_copy(vsS[:], B[4][:].rearrange("p (t c) -> p t c", t=TT)).then_inc(sem("v_S"), 1)
            dve.tensor_copy(vwS[:], B[5][:].rearrange("p (t c) -> p t c", t=TT)).then_inc(sem("v_S"), 1)
            dve.wait_ge(sem("cmp_kv"), 1)
            link(dve.memset(kcT[:], 0.0))
            link(dve.memset(vcS[:], 0.0))
            dve.tensor_copy(kcT[:, 0:NCMP], B[4][:, 0:NCMP]).then_inc(sem("cmp_out"), 1)
            for g in range(NG):
                dve.tensor_copy(vcS[g * NCP:g * NCP + NCMP, g * DH:(g + 1) * DH], B[5 + g][0:NCMP, 0:DH])\
                    .then_inc(sem("cmp_out"), 1)

            dve.memset(attnT[:], 0.0).then_inc(sem("attn_zero"), 1)
            for h in range(GH):
                dve.wait_ge(sem("la_act"), 3 * h + 3)
                link(dve.tensor_scalar(bT[:, h, :], B[h][:], vec("b_alpha", h), 0.0, ALU.add, ALU.min))
                link(dve.tensor_tensor(bT[:, h, :], bT[:, h, :], tmp[:, h % 2, :], ALU.subtract))
                dve.tensor_tensor_scan(bT[:, h, :], cst("reset"), bT[:, h, :], 0.0, ALU.mult, ALU.add)\
                    .then_inc(sem("b_ready"), 1)
            dve.wait_ge(sem("b_ready"), GH)
            dve.wait_ge(sem("attn_zero"), 1)

            def beside(p, it, per, t, bank, first):
                dve.wait_ge(sem("chunk_done"), it * per + (p.c0 + t + 1))
                dve.tensor_tensor(pj[:, bass.ds(it * per + (first + t), 1), :], bank[:].unsqueeze(1), nr[:].unsqueeze(1), ALU.mult)\
                    .then_inc(sem("bank_free"), 1)

            def gate_tile(h, t):
                beside(PH["r"], h, 2, t, B[3], GRR)

            with dve.Fori(0, GH) as h:
                bh = bT[:, bass.ds(h, 1), :].rearrange("p o (n c) -> p (o n) c", c=CH)
                dve.tensor_tensor(kd[:].rearrange("p (n c) -> p n c", c=CH),
                                  bh[:, :, CH - 1:CH].to_broadcast([P, NCH, CH]), bh, ALU.subtract)\
                    .then_inc(sem("gla_dif"), 1)
                dve.wait_ge(sem("gla_exp"), h * 4 + 3)
                dve.scalar_tensor_tensor(qe[:], pj[:, bass.ds(h + GQ, 1), :], DK ** -0.5, qe[:], ALU.mult, ALU.mult)\
                    .then_inc(sem("gla_qk"), 1)
                dve.tensor_tensor(ke[:], pj[:, bass.ds(h + GK, 1), :], ke[:], ALU.mult).then_inc(sem("gla_qk"), 1)
                dve.wait_ge(sem("gla_exp"), h * 4 + 4)
                dve.tensor_tensor(kd[:], pj[:, bass.ds(h + GK, 1), :], kd[:], ALU.mult).then_inc(sem("gla_qk"), 1)
                dve.wait_ge(sem("gla_s"), h + 1)
                dve.sem_inc(sem("dve_held"), 1)
                dve.copy_predicated(attnT[:], cst("causal64").bitcast(I32).unsqueeze(1).to_broadcast([P, TT, P]),
                                    B[5][:].rearrange("p (t c) -> p t c", t=TT)).then_inc(sem("gla_att"), 1)
                gate_tile(h, 0)
                for c in range(NCH - 1):
                    u = upd_bank(c)
                    dve.wait_ge(sem("gla_upd"), h * (NCH - 1) + min(NCH - 1, 4 * (c // 4) + 3 + c % 2))
                    if c == 0:
                        dve.tensor_copy(st[:, 0, :], u).then_inc(sem("gla_st"), 1)
                    else:
                        dve.wait_ge(sem("gla_st"), h * (NCH - 1) + c)
                        dve.scalar_tensor_tensor(st[:, c, :], st[:, c - 1, :], dec[:, c:c + 1], u, ALU.mult, ALU.add)\
                            .then_inc(sem("gla_st"), 1)
                dve.wait_ge(sem("gla_sq"), h * 2 + 2)
                dve.wait_ge(sem("gla_qk"), h * 3 + 3)
                dve.tensor_scalar(pj[:, bass.ds(h + GQ, 1), :], B[0][:].unsqueeze(1), vec("gla_g", 0), None, ALU.mult)
                dve.tensor_scalar(pj[:, bass.ds(h + GK, 1), :], B[1][:].unsqueeze(1), vec("gla_g", 1), None, ALU.mult).then_inc(sem("gla_raw"), 1)
                gate_tile(h, 1)
                dve.wait_ge(sem("gla_ms"), h + 1)
                dve.tensor_scalar(bT[:, bass.ds(h, 1), :], B[4][:], 1.0 / DV, EPS, ALU.mult, ALU.add)\
                    .then_inc(sem("gla_head"), 1)
            dve.wait_ge(sem("gla_head"), GH + 1)

            dve.wait_ge(sem("gates_ready"), 1)
            gview = gates[:].rearrange("p i (g r b) -> p r b i g", g=NG, r=NR)
            with dve.Fori(0, NR) as r:
                for g in range(NG):
                    dve.wait_ge(sem("cmp_s"), r * NG + g + 1)
                    dve.tensor_tensor(scS[:, :, g, :], B[2 + g][:, 0:TT * NCP].rearrange("p (i n) -> p i n", n=NCP),
                                      biasc[:, :, g, :], ALU.add).then_inc(sem("cmp_read"), 1)
                for k in range(NSQ + 1):
                    if k < NST:
                        g, br, i = GROUPS[k]
                        n = (i + 1) * P
                        dve.wait_ge(sem("nsa_s"), r * NST + (k + 1))
                        if k >= 2:
                            dve.wait_ge(sem("nsa_exp"), r * NST + (k - 1))
                        dve.sem_inc(sem("dve_held"), 1)
                        dve.tensor_tensor_reduce(out=sS[:, k % 2, 0:n], in0=B[2 + k % 2][:, 0:n], in1=biasg[g][:, S - n:S],
                                                 scale=-1.0, scalar=3e38, op0=ALU.add, op1=ALU.min,
                                                 accum_out=nmx[:, k:k + 1]).then_inc(sem("nsa_max"), 1)
                    if k == 0:
                        dve.wait_ge(sem("cmp_read"), r * NG + NG)
                        dve.tensor_reduce(cmx[:], scS[:], AX.X, ALU.max).then_inc(sem("cmp_dve"), 1)
                        dve.wait_ge(sem("cmp_dve"), r * 2 + 1)
                        dve.tensor_tensor(scS[:], scS[:], cmx[:].unsqueeze(3).to_broadcast([P, TT, NG, NCP]), ALU.subtract)\
                            .then_inc(sem("cmp_sub"), 1)
                    if k == 2:
                        dve.wait_ge(sem("cmp_exp"), r + 1)
                        dve.tensor_reduce(rsum[:, 2], scS[:], AX.X, ALU.add).then_inc(sem("cmp_dve"), 1)
                        dve.wait_ge(sem("cmp_dve"), r * 2 + 2)
                        dve.tensor_tensor(scS[:], scS[:], maskc, ALU.mult).then_inc(sem("cmp_p"), 1)
                    if k in M_OUT:
                        beside(PH["mgn"], r, 4, M_OUT.index(k), B[MBANK[M_OUT.index(k) % 2]], 0)
                    if k == NST:
                        dve.wait_ge(sem("nsa_max"), r * NST + (NST + 2))
                        dve.tensor_scalar(biasg[0], biasg[0], 0.5, None, ALU.mult)
                        dve.tensor_scalar(biasg[1], biasg[1], 0.5, None, ALU.mult)
                        dve.tensor_scalar(biasc, biasc, 0.5, None, ALU.mult).then_inc(sem("bias_half"), 1)
                        dve.wait_ge(sem("nsa_exp"), r * NST + NST)
                        dve.reciprocal(gsc[:], rsum[:]).then_inc(sem("nsa_dve"), 1)
                        dve.wait_ge(sem("nsa_dve"), r * 8 + 1)
                        for j, b in enumerate((1, 2, 0)):
                            dve.tensor_tensor(gsc[:, j], gsc[:, j], gview[:, bass.ds(r, 1), b].rearrange("p o i g -> p (o i) g"),
                                              ALU.mult).then_inc(sem("nsa_dve"), 1)
                    if k >= 1:
                        q = k - 1
                        n, rows = ((GROUPS[q][2] + 1) * P, P) if q < NST else (S, NG * NCP)
                        dve.wait_ge(sem("nsa_pT"), r * NSQ + (q + 3))
                        if q >= 2:
                            dve.wait_ge(sem("nsa_pv"), r * NSQ + (q - 1))
                        dve.tensor_copy(pT[0:rows, q % 2, 0:n], B[4 * (q % 2)][0:rows, 0:n]).then_inc(sem("nsa_pTS"), 1)
                dve.wait_ge(sem("nsa_dve"), r * 8 + 4)
                dve.wait_ge(sem("bias_half"), r + 1)
                oav = oacc[:].rearrange("p i (g d) -> p (i g) d", g=NG)
                otv = otmp[:].rearrange("p i (g d) -> p (i g) d", g=NG)

                def gated(j, dst):
                    return dve.tensor_tensor(dst, B[(5, 6, 3)[j]][:].rearrange("p (a d) -> p a d", d=DH),
                                             gsc[:, j].rearrange("p i g -> p (i g)").unsqueeze(2).to_broadcast([P, TT * NG, DH]),
                                             ALU.mult).then_inc(sem("nsa_dve"), 1)
                dve.wait_ge(sem("nsa_pv"), r * NSQ + NST)
                gated(0, oav)
                gated(1, otv)
                dve.wait_ge(sem("nsa_dve"), r * 8 + 6)
                dve.tensor_tensor(oav, oav, otv, ALU.add).then_inc(sem("nsa_dve"), 1)
                dve.wait_ge(sem("nsa_dve"), r * 8 + 7)
                dve.wait_ge(sem("nsa_pv"), r * NSQ + NSQ)
                gated(2, otv)
                dve.wait_ge(sem("nsa_dve"), r * 8 + 8)
                dve.tensor_tensor(oav, oav, otv, ALU.add).then_inc(sem("nsa_acc"), 1)
                dve.wait_ge(sem("gla_fin"), 2 * GH)
                beside(PH["mgn"], r, 4, 3, B[MBANK[1]], 0)

            low_of("og", lambda kt: pj[:, GRR + kt, :], KD)
            dve.wait_ge(sem("gates_mix"), 1)

            def times_gate(it, t, bank):
                s_ = sg[:, bass.ds(it * 4 + t, 1), :]
                dve.tensor_tensor(s_, bank[:], s_, ALU.mult).then_inc(sem("bank_free"), 1)
            evict(PH["pg"], times_gate)
            for kt in range(KD // 2):
                dve.wait_ge(sem("on_hi"), kt + 1)
                dve.tensor_tensor(onL[:, kt, :], pj[:, NQ + kt, :], onH[:, kt, :].bitcast(F32), ALU.subtract)\
                    .then_inc(sem("on_lo"), 1)
            dve.wait_ge(sem("gates_mix"), 2)

            def add_gated(it, t, bank):
                dve.wait_ge(sem("bank_free"), it * 4 + (NBANK + PH["pn"].t0 + t - 1))
                dve.tensor_tensor(tmp[:, t % 2, :].unsqueeze(1), bank[:].unsqueeze(1), sgn[:, bass.ds(it * 4 + t, 1), :], ALU.mult)\
                    .then_inc(sem("pn_mul"), 1)
                dve.wait_ge(sem("pn_mul"), it * 4 + (t + 1))
                s_ = sg[:, bass.ds(it * 4 + t, 1), :]
                dve.tensor_tensor(s_, s_, tmp[:, t % 2, :].unsqueeze(1), ALU.add).then_inc(sem("bank_free"), 1)
                dve.wait_ge(sem("mix1_hi"), it * 4 + (t + 1))
                dve.tensor_tensor(aL[:, bass.ds(it * 4 + t, 1), :], s_, aH[:, bass.ds(it * 4 + t, 1), :].bitcast(F32),
                                  ALU.subtract).then_inc(sem("mix1_lo"), 1)
            dve.wait_ge(sem("bank_free"), NBANK + PH["pn"].t0)
            evict(PH["pn"], add_gated)
            clear_sum(1)
            evict(PH["out1"], copy_and_square(zT, 1))

            def residual_and_low(src, gain, name, use, next_gain):
                for kt in range(KD):
                    if kt >= 2:
                        dve.wait_ge(sem(name), kt - 1)
                    dve.scalar_tensor_tensor(tmp[:, kt % 2, :], src[:, kt, :], vec(gain, kt), nr[:], ALU.mult, ALU.mult)\
                        .then_inc(sem(name + "_mul"), 1)
                    if kt >= 2:
                        low_of_x(use, next_gain, kt - 2)
                low_of_x(use, next_gain, KD - 2)
                low_of_x(use, next_gain, KD - 1)

            norm(2, 2, B[4])
            clear_sum(2)
            residual_and_low(zT, "g_mix_post", "res1", "h2", "g_ffn_pre")
            for kt in range(KD):
                add_square(2 * KD + kt)
            norm(3, 3, B[5])

            def swiglu(p, tag):
                with dve.Fori(0, p.nt // 4) as it:
                    for j in range(2):
                        dve.wait_ge(sem("chunk_done"), it * 4 + (p.c0 + 2 * j + 1))
                        dve.wait_ge(sem(tag + "_fL"), it * 2 + (j + 1))
                        dve.tensor_tensor(sq[:, j, :], B[(p.t0 + 2 * j) % NBANK][:], nr[:], ALU.mult)\
                            .then_inc(sem("bank_free"), 1)
                        dve.wait_ge(sem("bank_free"), it * 4 + (NBANK + p.t0 + 2 * j + 1))
                        dve.sem_inc(sem(tag + "_gate"), 1)
                        dve.wait_ge(sem("chunk_done"), it * 4 + (p.c0 + 2 * j + 2))
                        dve.tensor_tensor(tmp[:, j, :], B[(p.t0 + 2 * j + 1) % NBANK][:], nr[:], ALU.mult)\
                            .then_inc(sem("bank_free"), 1)
                        dve.wait_ge(sem("bank_free"), it * 4 + (NBANK + p.t0 + 2 * j + 2))
                        dve.wait_ge(sem(tag + "_silu"), it * 2 + (j + 1))
                        dve.tensor_tensor(tmp[:, j, :], tmp[:, j, :], sq[:, j, :], ALU.mult).then_inc(sem(tag + "_f"), 1)
                        dve.wait_ge(sem(tag + "_fH"), it * 2 + (j + 1))
                        dve.tensor_tensor(fL[:, bass.ds(it * 2 + j, 1), :], tmp[:, j, :].unsqueeze(1),
                                          fH[:, bass.ds(it * 2 + j, 1), :].bitcast(F32), ALU.subtract)\
                            .then_inc(sem(tag + "_fL"), 1)

            swiglu(PH["gu1"], "ff1")
            clear_sum(3)
            evict(PH["dn1"], copy_and_square(z2T, 3))
            norm(4, 4, B[4])
            clear_sum(4)
            residual_and_low(z2T, "g_ffn_post", "res2", "h3", "g_norm1")
            for kt in range(KD):
                add_square(4 * KD + kt)
            dve.wait_ge(sem("res2"), KD)
            dve.sem_inc(sem("ffn1_done"), 1)
            norm(5, 5, B[5])

            evict(PH["in2"], normed_to(pk), 2)
            dve.wait_ge(sem("up_zero"), 1)
            for j in range(4):
                dve.wait_ge(sem("glu_sig"), j + 1)
                dve.tensor_tensor(up[:, j, HP:HP + S], pk[:, j, :], pk[:, 4 + j, :], ALU.mult).then_inc(sem("conv_in"), 1)
            dve.wait_ge(sem("conv_in"), 4)
            for j in range(4):
                w = PV_AT["dw"] + j * TAPS
                dve.tensor_scalar(yT[:, j, :], up[:, j, 0:S], pv[:, w:w + 1], vec("dw_bias", j), ALU.mult, ALU.add)\
                    .then_inc(sem("conv_step"), 1)
            with dve.Fori(1, TAPS) as t:
                for j in range(4):
                    w = PV_AT["dw"] + j * TAPS
                    dve.wait_ge(sem("conv_step"), t * 4 + (j - 3))
                    dve.scalar_tensor_tensor(yT[:, j, :], up[:, j, bass.ds(t, S)], pv[:, bass.ds(t + w, 1)], yT[:, j, :],
                                             ALU.mult, ALU.add).then_inc(sem("conv_step"), 1)
            dve.wait_ge(sem("conv_step"), 4 * TAPS)
            dve.sem_inc(sem("conv_done"), 4)
            for j in range(8):
                dve.wait_ge(sem("sq_used"), 8 * 5 + j + 1)
                dve.tensor_scalar(nx[:], B[4 + j % 2][:], 1.0 / DH, EPS, ALU.mult, ALU.add).then_inc(sem("nx_ready"), 1)
                newton(6 + j)
                dve.scalar_tensor_tensor(pk[:, 8 + j, :], pk[:, 8 + j, :], vec("qn_g" if j < 4 else "kn_g"), nr[:],
                                         ALU.mult, ALU.mult).then_inc(sem("qk_normed"), 1)
                dve.wait_ge(sem("qk_normed"), j + 1)
            dve.wait_ge(sem("ln_sum"), 1)
            for j in range(4):
                dve.scalar_tensor_tensor(yT[:, j, :], B[6][:], -1.0 / S, yT[:, j, :], ALU.mult, ALU.add)\
                    .then_inc(sem("ln_cen"), 1)
            dve.wait_ge(sem("sq_used"), 8 * 6 + 4)
            dve.tensor_scalar(nx[:], B[7][:], 1.0 / S, EPS, ALU.mult, ALU.add).then_inc(sem("nx_ready"), 1)
            newton(14)
            for j in range(4):
                dve.tensor_tensor(yT[:, j, :], yT[:, j, :], nr[:], ALU.mult).then_inc(sem("conv_val"), 1)
            low_of("conv", lambda j: yT[:, j, :], 4)

            with dve.Fori(0, NH // 2) as j:
                for k in range(NS2 + 1):
                    if k < NS2:
                        dve.wait_ge(sem("na_s"), j * NS2 + (k + 1))
                        dve.wait_ge(sem("na_bias"), j * NS2 + (k + 1))
                        if k >= 2:
                            dve.wait_ge(sem("na_exp"), j * NS2 + (k - 1))
                        dve.sem_inc(sem("dve_held"), 1)
                        dve.tensor_tensor_reduce(out=s2[:, k % 2, :], in0=B[2 + k % 2][:, 0:GR * KC],
                                                 in1=bm[:, k % 2].rearrange("p r c -> p (r c)"), scale=-1.0, scalar=3e38,
                                                 op0=ALU.add, op1=ALU.min, accum_out=nm2[:, k:k + 1])\
                            .then_inc(sem("na_max"), 1)
                    if k >= 1:
                        q = k - 1
                        dve.wait_ge(sem("na_pT"), j * NS2 + (q + 3))
                        if q >= 2:
                            dve.wait_ge(sem("na_pv"), j * NS2 + (q - 1))
                        dve.tensor_copy(pT2[:, q % 2, :], B[4 + q % 2][:, 0:GR * KC]).then_inc(sem("na_pTS"), 1)
                dve.wait_ge(sem("na_exp"), j * NS2 + NS2)
                dve.reciprocal(rs2[:], rs2[:]).then_inc(sem("na_rec"), 1)
                dve.wait_ge(sem("na_rec"), j + 1)
                dve.wait_ge(sem("na_pv"), j * NS2 + NS2)
                dve.tensor_tensor(o2[:].rearrange("p i (f d) -> p f i d", f=2),
                                  B[6][:].rearrange("p (i f d) -> p f i d", i=TT, f=2),
                                  rs2[:].rearrange("p (f i) -> p f i", f=2).unsqueeze(3).to_broadcast([P, 2, TT, DH]),
                                  ALU.mult).then_inc(sem("na_norm"), 1)
                dve.wait_ge(sem("na_hi"), j + 1)
                dve.tensor_tensor(aL[:, bass.ds(j + 4, 1), :].rearrange("p o (r i c) -> p (o i) r c", r=GR, i=TT),
                                  B[7][:].rearrange("p (i r c) -> p i r c", i=TT, r=GR),
                                  aH[:, bass.ds(j + 4, 1), :].bitcast(F32).rearrange("p o (r i c) -> p (o i) r c", r=GR, i=TT),
                                  ALU.subtract).then_inc(sem("na_pair"), 1)

            def add_to_x(it, t, bank):
                x_ = xT[:, bass.ds(it * 4 + t, 1), :]
                dve.tensor_tensor(x_, bank[:].unsqueeze(1), x_, ALU.add).then_inc(sem("bank_free"), 1)

            def add_and_square(it, t, bank):
                add_to_x(it, t, bank)
                add_square(6 * KD + 4 + t, it)

            clear_sum(5)
            evict(PH["out2"], add_and_square)
            for kt in range(KD):
                low_of_x("h4", "g_norm2", kt)
            norm(6, 15, B[4])
            swiglu(PH["gu2"], "ff2")
            evict(PH["dn2"], add_to_x)
            for kt in range(1, KD, 2):
                dve.wait_ge(sem("outT"), kt + 1)
                dve.tensor_copy(os_[:, :, kt * P:(kt + 1) * P], B[4 + kt % 4][:].rearrange("p (t d) -> p t d", t=TT))\
                    .then_inc(sem("out_odd"), 1)


def lay_out(inputs):
    f = {k: np.asarray(v) for k, v in inputs.items()}
    f = {k: (v[0] if k != "x" else v[0]) for k, v in f.items()}

    def blocks(w):
        k, n = w.shape[0] // P, w.shape[1] // P
        return w.reshape(k, P, n, P).transpose(1, 2, 0, 3).reshape(P, -1)

    w = f["w_in"]
    z = np.zeros((D, P), np.float32)
    gw = 3 * NH
    at = np.cumsum([0, GH * DK, GH * DK, GH * DV, GH * DV, RANK, NH * DH] + 6 * [NG * DH] + [gw, D, D])
    sec = [w[:, at[i]:at[i + 1]] for i in range(len(at) - 1)]
    misc = np.concatenate([sec[4], z[:, :GATE_ROW - RANK], sec[12], z[:, :P - GATE_ROW - gw]], 1)
    nq = sec[5].reshape(D, NG, NR, DH).transpose(0, 2, 1, 3).reshape(D, NH * DH)
    k_c, v_c, k_s, v_s, k_w, v_w = sec[6:12]
    in1 = np.concatenate([sec[2], sec[0], sec[1], misc, nq, k_c, v_c, v_s, v_w, k_s, k_w, sec[3]], 1)
    pn = f["w_proj_nsa"].reshape(NG, NR, DH, D).transpose(1, 0, 2, 3).reshape(NH * DH, D)

    def pairs(g, u):
        return np.stack([g.reshape(D, KF, P), u.reshape(D, KF, P)], 2).reshape(D, 2 * FF)

    stream = np.concatenate(
        [blocks(a) for a in (in1, sec[13], sec[14], f["w_proj_gla"], pn, f["w_out"],
                             pairs(f["w_ffn_gate"], f["w_ffn_up"]), f["w_ffn_down"],
                             f["w_in_2"], f["w_out_2"], pairs(f["w_gate_2"], f["w_up_2"]), f["w_down_2"])]
        + [np.zeros((P, CW), np.float32)], 1)
    assert stream.shape[1] == NBLOCK * P + CW

    def cols(v):
        return v.reshape(-1, P).T

    def twice(v):
        return np.concatenate([v, v], 0)

    pvs = {"g_mix_pre": cols(f["norm_mix_pre"]), "g_mix_post": cols(f["norm_mix_post"]),
           "g_ffn_pre": cols(f["norm_ffn_pre"]), "g_ffn_post": cols(f["norm_ffn_post"]),
           "g_norm1": cols(f["norm1_g_2"]), "g_norm2": cols(f["norm2_g_2"]),
           "b_alpha": cols(f["gla_b_alpha"]), "gla_g": cols(f["gla_norm_g"]),
           "dw_bias": cols(f["dw_bias_2"]), "ln_g": cols(f["conv_ln_g_2"]), "ln_b": cols(f["conv_ln_b_2"]),
           "dw": f["dw_kernel_2"].reshape(TAPS, 4, P).transpose(2, 1, 0).reshape(P, 4 * TAPS),
           "qn_g": twice(f["q_norm_g_2"])[:, None], "kn_g": twice(f["k_norm_g_2"])[:, None],
           "pe_k": twice(f["nsa_cmp_pe_k"].T), "pe_v": twice(f["nsa_cmp_pe_v"].T)}
    pvec = np.concatenate([pvs[n] for n, _ in PV_COLS], 1)
    out = {"x": f["x"], "w": stream, "pv": pvec, "ct": constants(), "wa2": f["gla_w_alpha2"],
           "w1k": f["nsa_cmp_w1_k"], "w1v": f["nsa_cmp_w1_v"], "w2k": f["nsa_cmp_w2_k"], "w2v": f["nsa_cmp_w2_v"],
           "rpb": np.stack([f["rpb_2"][:, GR - 1 - r:2 * GR - 1 - r] for r in range(GR)]).reshape(GR, NH * GR, RB_C)}
    return {k: np.ascontiguousarray(v) for k, v in out.items()}


def kernel(**inputs):
    import concourse.bacc as bacc
    from concourse.bass_utils import run_bass_kernel_spmd

    nc = bacc.Bacc("TRN2", target_bir_lowering=False, num_devices=1)
    arrays, aps = {}, {}
    for name, a in lay_out(inputs).items():
        arrays[f"in_{name}"] = a
        aps[name] = nc.dram_tensor(f"in_{name}", a.shape, mybir.dt.from_np(a.dtype), kind="ExternalInput").ap()
    aps["out"] = nc.dram_tensor("out_x", (S, D), F32, kind="ExternalOutput").ap()
    two_blocks_kernel(nc, aps)
    r = run_bass_kernel_spmd(nc, [arrays], core_ids=[0])
    return np.asarray(r.results[0]["out_x"]).reshape(1, S, D)
```

```python
from contextlib import ExitStack

import numpy as np
import concourse.bass as bass
from concourse import mybir

ALU = mybir.AluOpType
ACT = mybir.ActivationFunctionType
F32 = mybir.dt.float32
F32R = mybir.dt.float32r
I32 = mybir.dt.int32
AX = mybir.AxisListType

P = 128
S = 512
TT = S // P
D = 1024
KD = D // P
FF = 2816
KF = FF // P
EPS = 1e-6
NEG = -1e30
GH, DK, DV, RANK, TAU, CH = 4, 128, 256, 16, 16.0, 64
NCH = S // CH
NH, NG, DH = 8, 2, 64
NR = NH // NG
CL, CST = 32, 16
NCMP = (S - CL) // CST + 1
NCP = 32
GATE_ROW = 32
GW, GR, NAC = 64, 8, 16
NACH = 16
QC = 16
KC = 32
TAPS = 31
HP = TAPS // 2
BM = 2 * KC - QC
RB_R, RB_C = 2 * GR - 1, 2 * NAC - 1
KEY_BASE = [min(max(QC * i - NAC // 2, 0), GW - KC) for i in range(4)]

GV, GQ, GK, MISC = 0, 8, 12, 16
KCT, VCT, VST, VWT, KST, KWT, NQ, GRR = 17, 18, 19, 20, 21, 22, 23, 27
IN1_EARLY, IN1_FIRST = 12, 15

PHASES = [("in1", GRR, KD), ("r", KD, KD), ("mgn", 2 * KD, KD), ("pg", KD, KD), ("pn", KD, KD // 2),
          ("out1", KD, KD), ("gu1", 2 * KF, KD), ("dn1", KD, KF),
          ("in2", 20, KD), ("out2n", KD, KD // 2), ("out2c", KD, KD // 2), ("gu2", 2 * KF, KD), ("dn2", KD, KF)]
CB = 8
CW = CB * P
NBANK = 4


class Phase:
    def __init__(self, name, nt, k, c0, t0, b0):
        self.name, self.nt, self.k, self.c0, self.t0, self.b0 = name, nt, k, c0, t0, b0
        if k == CB // 2:
            self.starts4 = [0, CB]
        else:
            self.starts4 = [n * k + j for n in range(4) for j in range(0, k, CB)]
        self.nc4 = len(self.starts4)
        self.nc = nt * self.nc4 // 4
        self.blocks4 = 4 * k

    def chunk_of(self, tile, k):
        if self.k == CB // 2:
            return tile // 2, (tile % 2) * self.k + k
        return tile * (self.nc4 // 4) + k // CB, k % CB

    def last_chunk(self, tile):
        return self.chunk_of(tile, self.k - 1)[0] + 1


def plan():
    out, c, t, b = {}, 0, 0, 0
    for name, nt, k in PHASES:
        p = Phase(name, nt, k, c, t, b)
        out[name] = p
        c, t, b = c + p.nc, t + nt, b + nt * k
    return out, c, t, b


PH, NCHUNK, NTILE, NBLOCK = plan()

PV_COLS = [("g_mix_pre", KD), ("g_mix_post", KD), ("g_ffn_pre", KD), ("g_ffn_post", KD),
           ("g_norm1", KD), ("g_norm2", KD), ("b_alpha", GH), ("gla_g", DV // P),
           ("dw_bias", 4), ("ln_g", 4), ("ln_b", 4), ("dw", 4 * TAPS), ("qn_g", 1), ("kn_g", 1),
           ("pe_k", CL), ("pe_v", CL)]
PV_AT, _n = {}, 0
for _name, _w in PV_COLS:
    PV_AT[_name] = _n
    _n += _w
NPV = _n
CT_COLS = [("ident", P), ("ones", P), ("sel", KD * NACH), ("reset", S), ("causal64", P), ("bias0", S), ("bias1", S),
           ("biasc", TT * NG * NCP), ("maskc", TT * NG * NCP), ("maskn", TT * KC)]
CT_AT, _n = {}, 0
for _name, _w in CT_COLS:
    CT_AT[_name] = (_n, _w)
    _n += _w
NCT = _n


def constants():
    c = np.zeros((P, NCT), np.float32)

    def put(name, a):
        at, w = CT_AT[name]
        c[:, at:at + w] = np.asarray(a, np.float32).reshape(P, w)

    p = np.arange(P)[:, None]
    put("ident", np.eye(P))
    put("ones", np.ones((P, P)))
    put("sel", np.arange(NACH)[None, None] == 2 * np.arange(KD)[None, :, None] + (p // DH)[:, :, None])
    t = np.arange(S)[None]
    put("reset", np.broadcast_to((t % CH != 0), (P, S)))
    m = np.arange(P)[None]
    put("causal64", (p <= m) & (p // CH == m // CH))
    d = t - (S - P) - p
    dist = np.where(d <= 0, d, NEG)
    for g in range(NG):
        put(f"bias{g}", dist * 2.0 ** -(g * NR + 1))
    n = np.arange(NCP)
    q = np.arange(TT)[None, :, None] * P + p[:, :, None]
    dc = (CST * n + CL - 1)[None, None] - q
    ok = (dc <= 0) & (n < NCMP)[None, None]
    put("biasc", np.stack([np.where(ok, dc, NEG) * 2.0 ** -(g * NR + 1) for g in range(NG)], 2))
    put("maskc", np.stack([ok] * NG, 2))
    cl = np.arange(P) % QC
    mask = np.zeros((P, TT, KC))
    for i in range(TT):
        col = QC * i + cl
        start = np.clip(col - NAC // 2, 0, GW - NAC)
        key = KEY_BASE[i] + np.arange(KC)
        mask[:, i] = np.where((key[None] >= start[:, None]) & (key[None] < start[:, None] + NAC), 0, NEG)
    put("maskn", mask)
    return c


def two_blocks_kernel(nc, A):
    with ExitStack() as ctx:
        def sb(name, shape, dt=F32, scope=ctx):
            return scope.enter_context(nc.sbuf_tensor(name, shape, dt))

        sems = {}

        def sem(name):
            if name not in sems:
                sems[name] = ctx.enter_context(nc.semaphore(name))
            return sems[name]

        xT = sb("xT", [P, KD, S])
        raw = sb("raw", [P, 2, CW])
        wH = sb("wH", [P, 2, CW], F32R)
        wL = sb("wL", [P, 2, CW], F32R)
        aH = sb("aH", [P, KD, S], F32R)
        aL = sb("aL", [P, KD, S], F32R)
        ct = sb("ct", [P, NCT])
        pv = sb("pv", [P, NPV])
        sq = sb("sq", [P, 2, S])
        tmp = sb("tmp", [P, 2, S])
        nx = sb("nx", [P, S])
        nr = sb("nr", [P, S])
        nt_ = sb("nt_", [P, S])
        ssum = sb("ssum", [P, S])

        sc1 = ExitStack()
        pj = sb("pj", [P, 35, S], F32, sc1)
        kcT = sb("kcT", [P, NCP], F32, sc1)
        vcS = sb("vcS", [NG * NCP, P], F32, sc1)
        vsS = sb("vsS", [P, TT, P], F32, sc1)
        vwS = sb("vwS", [P, TT, P], F32, sc1)
        gates = sb("gates", [P, TT, 3 * NH], F32, sc1)
        hid = sb("hid", [P, 2, NCMP], F32, sc1)
        w2k = sb("w2k", [P, DH], F32, sc1)
        w2v = sb("w2v", [P, DH], F32, sc1)
        wa2 = sb("wa2", [RANK, GH * DK], F32, sc1)
        with ExitStack() as early:
            kin_ = sb("kin", [P, 2, CL, NCMP], F32, early)
            w1k = sb("w1k", [P, CL, DH], F32, early)
            w1v = sb("w1v", [P, CL, DH], F32, early)
        kin = [kin_[:, i] for i in range(2)]
        xs = pj[:, 27:35, :].rearrange("p a s -> p (a s)").rearrange("p (t d) -> p t d", t=TT)
        with ExitStack() as gla:
            bT = sb("bT", [P, GH, S], F32, gla)
            qe = sb("qe", [P, S], F32, gla)
            ke = sb("ke", [P, S], F32, gla)
            kd = sb("kd", [P, S], F32, gla)
            kdS = sb("kdS", [P, TT, P], F32, gla)
            vS = sb("vS", [P, TT, DV], F32, gla)
            attnT = sb("attnT", [P, TT, P], F32, gla)
            st = sb("st", [P, NCH - 1, DV], F32, gla)
            dec = sb("dec", [P, NCH], F32, gla)
        with ExitStack() as nsa:
            sb("bT_kept", [P, GH, S], F32, nsa)
            qst = sb("qst", [P, S], F32, nsa)
            sS = sb("sS", [P, 2, S], F32, nsa)
            pS = sb("pS", [P, 2, S], F32, nsa)
            pT = sb("pT", [P, 2, S], F32, nsa)
            scS = sb("scS", [P, TT, NG, NCP], F32, nsa)
            cmx = sb("cmx", [P, TT, NG], F32, nsa)
            nmx = sb("nmx", [P, 2 * NG * TT], F32, nsa)
            rsum = sb("rsum", [P, 3, TT, NG], F32, nsa)
            gsc = sb("gsc", [P, 3, TT, NG], F32, nsa)
            oacc = sb("oacc", [P, TT, P], F32, nsa)
            otmp = sb("otmp", [P, TT, P], F32, nsa)
        with ExitStack() as mrg:
            onH = sb("onH", [P, KD // 2, S], F32R, mrg)
            onL = sb("onL", [P, KD // 2, S], F32R, mrg)
        rs4 = pj[:, KCT:KCT + GH, :]
        sg = pj[:, 0:KD, :]
        sgn = pj[:, KD:2 * KD, :]
        zT = pj[:, KD:2 * KD, :]
        sc1.close()
        with ExitStack() as ffn:
            fH = sb("fH", [P, KF, S], F32R, ffn)
            fL = sb("fL", [P, KF, S], F32R, ffn)
            z2T = sb("z2T", [P, KD, S], F32, ffn)
        with ExitStack() as sc2:
            pk = sb("pk", [P, 20, S], F32, sc2)
            up = sb("up", [P, 4, S + 2 * HP], F32, sc2)
            yT = sb("yT", [P, 4, S], F32, sc2)
            VS = sb("VS", [P, TT, 2, 4 * P], F32, sc2)
            bt = sb("bt", [P, NH, GR, BM], F32, sc2)
            bm = sb("bm", [P, 3, GR, KC], F32, sc2)
            q2 = sb("q2", [P, 2, S], F32, sc2)
            k2 = sb("k2", [P, 2, S], F32, sc2)
            sp2 = sb("sp2", [P, 6, GR * KC], F32, sc2)
            s2, p2 = sp2[:, 0:3], sp2[:, 3:6]
            vst = sp2[:, 0:TT]
            pT2 = sb("pT2", [P, 2, GR * KC], F32, sc2)
            nm2 = sb("nm2", [P, 16], F32, sc2)
            rs2 = sb("rs2", [P, 16], F32, sc2)
            spread = sb("spread", [NACH, NACH * DH], F32, sc2)
            o2 = nt_[:].rearrange("p (i d) -> p i d", i=TT)
        os_ = z2T[:].rearrange("p a s -> p (a s)").rearrange("p (t d) -> p t d", t=TT)

        B = [ctx.enter_context(nc.psum_tensor(f"bank{i}", [P, S], F32)) for i in range(8)]

        def cst(name):
            at, w = CT_AT[name]
            return ct[:, at:at + w]

        def vec(name, i=0):
            return pv[:, PV_AT[name] + i:PV_AT[name] + i + 1]

        ident, ones = cst("ident"), cst("ones")
        biasg = [cst("bias0"), cst("bias1")]
        biasc = cst("biasc").rearrange("p (i g n) -> p i g n", g=NG, n=NCP)
        maskc = cst("maskc").rearrange("p (i g n) -> p i g n", g=NG, n=NCP)
        maskn = cst("maskn").rearrange("p (i c) -> p i c", c=KC)
        GROUPS = [(g, br, i) for g in range(NG) for br in range(2) for i in range(TT)]
        NST = len(GROUPS)
        NSQ = NST + 1
        STEPS2 = [(pp, hf, i) for pp in range(2) for hf in range(2) for i in range(TT)]
        NS2 = len(STEPS2)

        def upd_bank(c):
            half = (c // 2) % 2
            return (B[6], B[7], B[4], B[2])[2 * (c // 4) + c % 2][:, half * DV:(half + 1) * DV]

        OUT_AFTER = [[t] + ([3 + t] if t else []) for t in range(4)] + [[KD - 1]]
        OUT_ORDER = [kt for a in OUT_AFTER for kt in a]
        OUT_BANK = {kt: 4 + n % 4 for n, kt in enumerate(OUT_ORDER)}
        TQ, TV = 2, 2
        T_V, T_N = 1 + 8 * TQ, 1 + 8 * TQ + 3 * TV
        TN = (TAPS - T_N) // 2
        ACT_TAPS, POOL_TAPS = (1, 4, 7, 10), (4, 7, 10, 13)
        assert T_N + 2 * TN == TAPS and TN == len(ACT_TAPS)
        ALPHA_BANK = (4, 5, 4, 6)
        R_UNITS = (4, 4, 5, 3)
        M_START, M_STEP, M_END = 3, (2, 2, 1, 1), 5
        M_OUT = (3, 9, 14)
        MBANK = (1, 7)

        block = ctx.enter_context(nc.Block())

        @block.sync
        def _(sp):

            def load(c_slot, c_wait, block0):
                if c_wait is not None:
                    sp.wait_ge(sem("w_lo"), c_wait)
                sp.dma_start(raw[:, c_slot, :], A["w"][:, bass.ds(block0 * P, CW)])\
                    .then_inc(sem(f"w_landed{c_slot}"), 16)

            for p in PH.values():
                n4 = p.nt // 4
                if p.c0 == 0:
                    load(0, None, p.starts4[0])
                    for t in range(TT):
                        sp.dma_start(xs[:, t, :], A["x"][t * P:(t + 1) * P, :]).then_inc(sem(f"x_landed{t}"), 16)
                    for j in range(1, 4):
                        load(j % 2, j - 1 if j >= 2 else None, p.starts4[j])
                with sp.Fori(1 if p.c0 == 0 else 0, n4) as it:
                    for j in range(p.nc4):
                        load((p.c0 + j) % 2, it * p.nc4 + (p.c0 + j - 1), it * p.blocks4 + (p.b0 + p.starts4[j]))
                for j in range(p.nt % 4):
                    c = n4 * 4 + j
                    load((p.c0 + c) % 2, p.c0 + c - 1, p.b0 + c * CB)
            for kt in OUT_ORDER:
                sp.wait_ge(sem("out_odd" if kt % 2 else "out_even"), kt // 2 + 1)
                c = slice(kt * P, (kt + 1) * P)
                sp.dma_start(A["out"].rearrange("(t p) d -> p t d", p=P)[:, :, c], os_[:, :, c]).then_inc(sem("stored"), 16)
            sp.wait_ge(sem("stored"), 16 * KD)

        @block.gpsimd
        def _(pool):
            def low(c_slot, n):
                pool.wait_ge(sem("w_hi"), n)
                pool.tensor_tensor(wL[:, c_slot, :], raw[:, c_slot, :], wH[:, c_slot, :].bitcast(F32),
                                   ALU.subtract).then_inc(sem("w_lo"), 1)

            def lows(c0, c1):
                with pool.Fori(0, (c1 - c0) // 2) as it:
                    for j in range(2):
                        low((c0 + j) % 2, it * 2 + (c0 + j + 1))
                if (c1 - c0) % 2:
                    low((c1 - 1) % 2, c1)

            def add_residual(name):
                for kt in range(KD):
                    pool.wait_ge(sem(name + "_mul"), kt + 1)
                    pool.tensor_tensor(xT[:, kt, :], xT[:, kt, :], tmp[:, kt % 2, :], ALU.add).then_inc(sem(name), 1)

            i2 = PH["in2"].c0
            na0 = PH["out2n"].c0 + 2
            m = PH["mgn"].c0 + 2
            lows(0, m)
            pool.wait_ge(sem("r_silu"), 1)
            links = 0

            def linked(ins):
                nonlocal links
                links += 1
                ins.then_inc(sem("pool_link"), 1)
                pool.wait_ge(sem("pool_link"), links)

            for h in range(GH):
                pool.wait_ge(sem("gla_rs"), 2)
                rs, t = rs4[:, h, :], nx[:]
                linked(pool.tensor_tensor(t, rs, rs, ALU.mult))
                linked(pool.tensor_tensor(t, t, bT[:, h, :], ALU.mult))
                linked(pool.tensor_scalar(t, t, -0.5, 1.5, ALU.mult, ALU.add))
                linked(pool.tensor_tensor(rs, rs, t, ALU.mult))
                for e in range(2):
                    o = pj[:, GQ + h if e == 0 else GK + h, :]
                    r_ = pj[:, GRR + 2 * h + e, :]
                    linked(pool.tensor_tensor(o, o, rs, ALU.mult))
                    pool.tensor_tensor(r_, o, r_, ALU.mult).then_inc(sem("gla_fin"), 1)
                if h < GH - 1:
                    low((m + h) % 2, m + h + 1)
            pool.wait_ge(sem("gla_fin"), 2 * GH)
            lows(m + GH - 1, PH["gu1"].c0 + 2)
            add_residual("res1")
            lows(PH["gu1"].c0 + 2, i2 + 2)
            add_residual("res2")
            lows(i2 + 2, i2 + 6)
            pool.wait_ge(sem("ffn1_done"), 1)
            pool.memset(bt[:], 0.0).then_inc(sem("bt_zero"), 1)
            pool.memset(up[:], 0.0).then_inc(sem("up_zero"), 1)
            lows(i2 + 6, i2 + 10)
            def add_taps(base, t, n):
                for u in range(t, t + n):
                    pool.wait_ge(sem("conv_mul"), base + (u + 1))
                    pool.wait_ge(sem("conv_add"), base + (u + 1))
                    pool.tensor_tensor(yT[:, 3, :], yT[:, 3, :], tmp[:, u % 2, :], ALU.add)\
                        .then_inc(sem("conv_add"), 1)
            with pool.Fori(0, 4) as it:
                for j in range(2):
                    low((i2 + j) % 2, it * 2 + (i2 + 10 + j + 1))
                    add_taps(it * (2 * TQ), 1 + TQ * j, TQ)
            for j in range(4):
                low((i2 + j) % 2, i2 + 18 + j + 1)
                if j < 3:
                    add_taps(0, T_V + TV * j, TV)
            pool.wait_ge(sem("bt_landed"), 16 * QC)
            with pool.Fori(0, 2) as it:
                for m, (pp, hf, i) in enumerate(STEPS2):
                    off = KEY_BASE[i] - QC * i + NAC
                    pool.wait_ge(sem("na_max"), it * NS2 + max(0, m - 2) + 1)
                    pool.sem_inc(sem("pool_held"), 1)
                    pool.tensor_tensor(bm[:, m % 3], bt[:, bass.ds(it * 4 + (pp * 2 + hf), 1), :, off:off + KC],
                                       maskn[:, i:i + 1, :].to_broadcast([P, GR, KC]), ALU.add)\
                        .then_inc(sem("na_bias"), 1)
                    if m in POOL_TAPS:
                        add_taps(it * TN, T_N + POOL_TAPS.index(m), 1)
            lows(na0, NCHUNK)

        @block.scalar
        def _(act):
            act.dma_start(ct[:, 0:2 * P], A["ct"][:, 0:2 * P]).then_inc(sem("ones_landed"), 16)
            act.dma_start(pv[:], A["pv"]).then_inc(sem("pv_landed"), 16)
            act.preload_act_table_set("natural_log_exp_and_others")

            def high(c_slot, landed, used):
                act.wait_ge(sem(f"w_landed{c_slot}"), landed)
                if used is not None:
                    act.wait_ge(sem("chunk_done"), used)
                act.activation(wH[:, c_slot, :], raw[:, c_slot, :], ACT.Copy).then_inc(sem("w_hi"), 1)

            def ahead(p, j, it=0, last=False):
                if last and p.c0 + p.nc4 * (p.nt // 4 - 1) + j + 2 >= NCHUNK:
                    act.wait_ge(sem("chunk_done"), it * p.nc4 + (p.c0 + j + 1))
                    return
                s = (p.c0 + j) % 2
                n = (p.c0 + j) // 2 + 2
                act.wait_ge(sem(f"w_landed{s}"), it * (p.nc4 * 8) + 16 * n)
                act.wait_ge(sem("chunk_done"), it * p.nc4 + (p.c0 + j + 1))
                act.activation(wH[:, s, :], raw[:, s, :], ACT.Copy).then_inc(sem("w_hi"), 1)

            def ahead_beside(p, j, it, per):
                s = (p.c0 + j) % 2
                act.wait_ge(sem(f"w_landed{s}"), it * (per * 8) + 16 * ((p.c0 + j) // 2 + 2))
                act.wait_ge(sem("chunk_done"), it * per + (p.c0 + j + 1))
                act.activation(wH[:, s, :], raw[:, s, :], ACT.Copy).then_inc(sem("w_hi"), 1)

            def gemm(p, evict=None, mid=None):
                def body(it, tiles, base, last=False, mid=None):
                    q = 0
                    for t in range(tiles):
                        while q < p.last_chunk(t):
                            ahead(p, base * p.nc4 // 4 + q, it, last)
                            q += 1
                        if mid is not None and t == 1:
                            mid()
                        if evict is not None:
                            evict(it, base + t)
                n4 = p.nt // 4
                if mid is not None:
                    body(0, 4, 0, mid=mid)
                    with act.Fori(1, n4) as it:
                        body(it, 4, 0)
                elif p.name == PHASES[-1][0]:
                    with act.Fori(0, n4 - 1) as it:
                        body(it, 4, 0)
                    body(n4 - 1, 4, 0, True)
                else:
                    with act.Fori(0, n4) as it:
                        body(it, 4, 0)
                if p.nt % 4:
                    body(0, p.nt % 4, n4 * 4)

            def square(n, src, it=0, wait=None):
                if wait is not None:
                    act.wait_ge(*wait)
                if n >= 2:
                    act.wait_ge(sem("sq_used"), it * 4 + (n - 1))
                act.activation(sq[:, n % 2, :], src(), ACT.Square).then_inc(sem("sq_ready"), 1)

            def rsqrt(n, rows=P, r=nr):
                act.wait_ge(sem("nx_ready"), n)
                act.activation(r[0:rows, :], nx[0:rows, :], ACT.Ln).then_inc(sem("ln_ready"), 1)
                act.wait_ge(sem("ln_ready"), n)
                act.activation(r[0:rows, :], r[0:rows, :], ACT.Exp, scale=-0.5).then_inc(sem("nr_ready"), 1)

            def high_of_x(use, gain, ready=None, norm=None):
                for kt in range(KD):
                    if ready is not None:
                        act.wait_ge(sem(ready), kt + 1)
                    act.activation(aH[:, kt, :], xT[:, kt, :], ACT.Copy, scale=vec(gain, kt))\
                        .then_inc(sem(use + "_hi"), 1)
                for kt in range(KD if norm is not None else 0):
                    square(norm * KD + kt, lambda: xT[:, kt, :])

            high(0, 16, None)
            act.wait_ge(sem("x_landed3"), 16)
            act.dma_start(ct[:, 2 * P:], A["ct"][:, 2 * P:]).then_inc(sem("ct_landed"), 16)
            act.dma_start(wa2[:], A["wa2"]).then_inc(sem("small_landed"), 16)
            for name, dst in (("w1k", w1k), ("w1v", w1v)):
                for g in range(NG):
                    act.dma_start(dst[g * DH:(g + 1) * DH], A[name].rearrange("(l d) o -> d l o", d=DH))\
                        .then_inc(sem("small_landed"), 16)
            for name, dst in (("w2k", w2k), ("w2v", w2v)):
                for g in range(NG):
                    act.dma_start(dst[g * DH:(g + 1) * DH], A[name]).then_inc(sem("small_landed"), 16)


            high(1, 16, None)
            act.wait_ge(sem("pv_landed"), 16)
            high_of_x("h1", "g_mix_pre", "xT_ready", 0)
            def group(p, base, tiles=4):
                for q in range(tiles * p.nc4 // 4):
                    ahead(p, base * p.nc4 // 4 + q)

            p = PH["in1"]
            ahead(p, 0)
            ahead(p, 1)
            rsqrt(1)
            ahead(p, 2)
            ahead(p, 3)
            with act.Fori(1, 3) as it:
                for j in range(4):
                    ahead(p, j, it)

            act.wait_ge(sem("gate_T"), 1)
            act.activation(gates[:], B[6][:].rearrange("p (t c) -> p t c", t=TT)[:, :, GATE_ROW:GATE_ROW + 3 * NH],
                           ACT.Sigmoid).then_inc(sem("gates_ready"), 1)
            group(p, 12)
            act.wait_ge(sem("cmp_hid"), 1)
            for i in range(2):
                act.activation(hid[:, i, :], B[7][:, i * 64:i * 64 + NCMP], ACT.Silu).then_inc(sem("hid_ready"), 1)

            act.preload_act_table_set("natural_log_exp_and_others")

            def log_gate(h):
                act.wait_ge(sem("alpha_z"), h + 1)
                if h >= 2:
                    act.wait_ge(sem("b_ready"), h - 1)
                lnb = tmp[:, h % 2, :]
                act.activation(lnb, B[ALPHA_BANK[h]][:], ACT.Abs, bias=vec("b_alpha", h)).then_inc(sem("la_act"), 1)
                act.wait_ge(sem("la_act"), 3 * h + 1)
                act.activation(lnb, lnb, ACT.Exp, scale=-1.0).then_inc(sem("la_act"), 1)
                act.wait_ge(sem("la_act"), 3 * h + 2)
                act.activation(lnb, lnb, ACT.Ln, bias=1.0).then_inc(sem("la_act"), 1)

            log_gate(0)
            log_gate(1)
            group(p, 16)
            group(p, 20)
            log_gate(2)
            log_gate(3)
            group(p, 24, 3)

            act.wait_ge(sem("bank_free"), NBANK + PH["r"].t0)
            act.wait_ge(sem("b_ready"), GH)
            with act.Fori(0, GH) as h:
                bh = bT[:, bass.ds(h, 1), :]
                act.wait_ge(sem("gla_head"), h + 1)
                act.activation(qe[:], bh, ACT.Exp, scale=1 / TAU).then_inc(sem("gla_exp"), 1)
                act.activation(ke[:], bh, ACT.Exp, scale=-1 / TAU).then_inc(sem("gla_exp"), 1)
                act.activation(dec[:], bT[:, bass.ds(h, 1), CH - 1::CH], ACT.Exp, scale=1 / TAU)\
                    .then_inc(sem("gla_exp"), 1)
                act.activation(tmp[:], pj[:, bass.ds(h * 2 + GV, 2), :], ACT.Copy).then_inc(sem("gla_v"), 1)
                act.wait_ge(sem("gla_dif"), h + 1)
                act.activation(kd[:], kd[:], ACT.Exp, scale=1 / TAU).then_inc(sem("gla_exp"), 1)
                act.wait_ge(sem("gla_vT"), h + 1)
                for i in range(2):
                    act.activation(vS[:, 2 * i:2 * i + 2, :], B[i][:].rearrange("p (t e) -> p t e", t=2), ACT.Copy)\
                        .then_inc(sem("gla_vS"), 1)
                act.wait_ge(sem("gla_kdT"), h + 1)
                act.activation(kdS[:], B[4][:].rearrange("p (t e) -> p t e", t=TT), ACT.Copy)\
                    .then_inc(sem("gla_kdS"), 1)
                ahead_beside(PH["r"], 0, h, 2)
                for e in range(2):
                    act.wait_ge(sem("gla_o"), h * 2 + (e + 1))
                    act.activation(sq[:, e, :], B[e][:], ACT.Square).then_inc(sem("gla_sq"), 1)
                ahead_beside(PH["r"], 1, h, 2)
            act.wait_ge(sem("gla_head"), GH + 1)
            act.activation(pj[:, GRR:GRR + KD, :], pj[:, GRR:GRR + KD, :], ACT.Silu).then_inc(sem("r_silu"), 1)
            act.preload_act_table_set("natural_log_exp_and_others")
            act.activation(rs4, bT[:], ACT.Ln).then_inc(sem("gla_rs"), 1)
            act.wait_ge(sem("gla_rs"), 1)
            act.activation(rs4, rs4, ACT.Exp, scale=-0.5).then_inc(sem("gla_rs"), 1)

            with act.Fori(0, NR) as r:
                act.activation(qst[:], pj[:, bass.ds(r + NQ, 1), :], ACT.Copy, scale=DH ** -0.5)\
                    .then_inc(sem("nsa_q"), 1)
                for k, (g, br, i) in enumerate(GROUPS):
                    n = (i + 1) * P
                    act.wait_ge(sem("nsa_max"), r * NST + (k + 3))
                    if k:
                        act.wait_ge(sem("nsa_pT"), r * NSQ + (k + 1))
                    act.activation(pS[:, k % 2, 0:n], sS[:, k % 2, 0:n], ACT.Exp, scale=-1.0, bias=nmx[:, k:k + 1],
                                   accum_out=rsum[:, br, i, g:g + 1]).then_inc(sem("nsa_exp"), 1)
                    if k == 0:
                        act.wait_ge(sem("cmp_sub"), r + 1)
                        act.activation(scS[:], scS[:], ACT.Exp).then_inc(sem("cmp_exp"), 1)
                    if k in M_OUT:
                        ahead_beside(PH["mgn"], M_OUT.index(k), r, 4)
                ahead_beside(PH["mgn"], 3, r, 4)
                act.wait_ge(sem("nsa_oT"), r + 1)
                act.sem_inc(sem("act_held"), 1)
                act.activation(pj[:, bass.ds(r + NQ, 1), :], B[4][:].unsqueeze(1), ACT.Copy).then_inc(sem("nsa_out"), 1)

            act.wait_ge(sem("gla_fin"), 2 * GH)
            for kt in range(KD):
                act.activation(aH[:, kt, :], pj[:, GRR + kt, :], ACT.Copy).then_inc(sem("og_hi"), 1)

            def gate(dst, tiles):
                act.wait_ge(sem("bank_free"), NBANK + PH["mgn"].t0 + tiles)
                act.activation(dst, dst, ACT.Sigmoid).then_inc(sem("gates_mix"), 1)

            gate(sg, KD)

            def gate_and_split():
                gate(sgn, 2 * KD)
                for kt in range(KD // 2):
                    act.activation(onH[:, kt, :], pj[:, NQ + kt, :], ACT.Copy).then_inc(sem("on_hi"), 1)
            gemm(PH["pg"], mid=gate_and_split)

            def high_mix(it, t):
                act.wait_ge(sem("bank_free"), it * 4 + (NBANK + PH["pn"].t0 + t + 1))
                act.activation(aH[:, bass.ds(it * 4 + t, 1), :], sg[:, bass.ds(it * 4 + t, 1), :], ACT.Copy)\
                    .then_inc(sem("mix1_hi"), 1)
            gemm(PH["pn"], high_mix)

            def square_of(p, u, src):
                def after(it, t):
                    square(u * KD + t, lambda: src[:, bass.ds(it * 4 + t, 1), :].rearrange("p o s -> p (o s)"), it,
                           (sem("bank_free"), it * 4 + (NBANK + p.t0 + t + 1)))
                return after

            gemm(PH["out1"], square_of(PH["out1"], 1, zT))
            rsqrt(2)
            high_of_x("h2", "g_ffn_pre", "res1", 2)

            def swiglu(p, tag, norm):
                def silu(it, j):
                    act.wait_ge(sem(tag + "_gate"), it * 2 + (j + 1))
                    act.activation(sq[:, j, :], sq[:, j, :], ACT.Silu).then_inc(sem(tag + "_silu"), 1)

                def high_f(it, j):
                    act.wait_ge(sem(tag + "_f"), it * 2 + (j + 1))
                    act.activation(fH[:, bass.ds(it * 2 + j, 1), :], tmp[:, j, :].unsqueeze(1), ACT.Copy)\
                        .then_inc(sem(tag + "_fH"), 1)
                ahead(p, 0)
                ahead(p, 1)
                rsqrt(norm)
                ahead(p, 2)
                silu(0, 0)
                high_f(0, 0)
                silu(0, 1)
                ahead(p, 3)
                high_f(0, 1)
                with act.Fori(1, p.nt // 4) as it:
                    for j in range(2):
                        ahead(p, 2 * j, it)
                        silu(it, j)
                        ahead(p, 2 * j + 1, it)
                        high_f(it, j)

            swiglu(PH["gu1"], "ff1", 3)
            gemm(PH["dn1"], square_of(PH["dn1"], 3, z2T))
            act.preload_act_table_set("natural_log_exp_and_others")
            rsqrt(4)

            high_of_x("h3", "g_norm1", "res2", 4)

            p = PH["in2"]

            for t in range(8):
                ahead(p, t)
                if t == 1:
                    rsqrt(5)
            act.wait_ge(sem("bank_free"), NBANK + p.t0 + 8)
            for j in range(4):
                act.activation(pk[:, 4 + j, :], pk[:, 4 + j, :], ACT.Sigmoid).then_inc(sem("glu_sig"), 1)
            w = PV_AT["dw"] + 3 * TAPS
            act.wait_ge(sem("conv_in"), 4)
            act.activation(yT[:, 3, :], up[:, 3, 0:S], ACT.Identity, scale=pv[:, w:w + 1], bias=vec("dw_bias", 3))\
                .then_inc(sem("conv_mul"), 1)

            def taps(base, t, n):
                for u in range(t, t + n):
                    act.wait_ge(sem("conv_add"), base + u)
                    act.sem_inc(sem("act_held"), 1)
                    act.activation(tmp[:, u % 2, :], up[:, 3, bass.ds(base + u, S)], ACT.Copy,
                                   scale=pv[:, bass.ds(base + (w + u), 1)]).then_inc(sem("conv_mul"), 1)

            with act.Fori(0, 4) as it:
                for j in range(2):
                    ahead_beside(p, 8 + j, it, 2)
                    taps(it * (2 * TQ), 1 + TQ * j, TQ)
                    act.wait_ge(sem("bank_free"), it * 2 + (NBANK + p.t0 + 9 + j))
                    act.wait_ge(sem("sq_used"), it * 2 + (5 * KD + j - 1))
                    act.sem_inc(sem("act_held"), 1)
                    act.activation(sq[:, j, :], pk[:, bass.ds(it * 2 + (8 + j), 1), :].rearrange("p o s -> p (o s)"), ACT.Square)\
                        .then_inc(sem("sq_ready"), 1)

            def spread_values(j):
                act.wait_ge(sem("bank_free"), NBANK + p.t0 + 17 + j)
                if j:
                    act.wait_ge(sem("na_VT"), j)
                for i in range(TT):
                    act.activation(vst[:, i, :].rearrange("p (r c) -> p r c", r=GR),
                                   pk[:, 16 + j, :].rearrange("p (r c) -> p r c", r=GR)[:, :, KEY_BASE[i]:KEY_BASE[i] + KC],
                                   ACT.Copy).then_inc(sem("na_vst"), 1)

            def values(j):
                act.wait_ge(sem("na_VT"), j + 1)
                for b in range(2):
                    act.activation(VS[:, 2 * b:2 * b + 2, :, j * P:(j + 1) * P],
                                   B[6 + b][:].rearrange("p (i v d) -> p i v d", i=2, v=2), ACT.Copy).then_inc(sem("na_VS"), 1)

            ahead(p, 16)
            taps(0, T_V, TV)
            act.wait_ge(sem("bt_zero"), 1)
            for c in range(QC):
                act.dma_start(bt[c::QC, :, :, c + 1:c + 1 + RB_C].rearrange("p h r c -> p (h r) c"), A["rpb"])\
                    .then_inc(sem("bt_landed"), 16)
            act.dma_start(spread[:], A["spread"]).then_inc(sem("spread_landed"), 16)
            ahead(p, 17)
            taps(0, T_V + TV, TV)
            spread_values(0)
            taps(0, T_V + 2 * TV, TV)
            values(0)
            spread_values(1)
            ahead(p, 18)
            values(1)
            act.preload_act_table_set("natural_log_exp_and_others")
            rsqrt(6, NACH, ssum)
            spread_values(2)
            ahead(p, 19)
            values(2)
            spread_values(3)
            values(3)

            act.wait_ge(sem("qk_normed"), 8)
            with act.Fori(0, 2) as it:
                def queries_keys(pp):
                    act.activation(q2[:, pp, :].rearrange("p (i r c) -> p i r c", i=TT, r=GR),
                                   pk[:, bass.ds(it * 2 + (pp + 8), 1), :].rearrange("p o (r i c) -> p (o i) r c", r=GR, i=TT),
                                   ACT.Copy, scale=DH ** -0.5).then_inc(sem("na_qk"), 1)
                    act.activation(k2[:, pp, :].unsqueeze(1), pk[:, bass.ds(it * 2 + (pp + 12), 1), :], ACT.Copy)\
                        .then_inc(sem("na_qk"), 1)

                def high_out(pp):
                    act.wait_ge(sem("na_oT"), it * 2 + pp + 1 + 1)
                    act.sem_inc(sem("act_held"), 1)
                    act.activation(aH[:, bass.ds(it * 2 + (pp + 4), 1), :].rearrange("p o (r i c) -> p (o i) r c", r=GR, i=TT),
                                   B[0][:].rearrange("p (i r c) -> p i r c", i=TT, r=GR), ACT.Copy)\
                        .then_inc(sem("na_hi"), 1)
                queries_keys(0)
                for m in range(NS2):
                    act.wait_ge(sem("na_max"), it * NS2 + (m + 1) + 1)
                    act.wait_ge(sem("na_pT"), it * NS2 + max(0, m - 2) + 1)
                    act.activation(p2[:, m % 3, :], s2[:, m % 3, :], ACT.Exp, scale=-1.0, bias=nm2[:, m:m + 1],
                                   accum_out=rs2[:, m:m + 1]).then_inc(sem("na_exp"), 1)
                    if m == 2:
                        queries_keys(1)
                    if m in ACT_TAPS:
                        taps(it * TN, T_N + ACT_TAPS.index(m), 1)
                    if m == 14:
                        high_out(0)
                high_out(1)

            p = PH["out2n"]
            ahead(p, 0)
            for j in range(4):
                square(6 * KD + j, lambda: yT[:, j, :], wait=(sem("ln_cen"), j + 1))
            ahead(p, 1)
            ahead(p, 2)
            rsqrt(7)
            ahead(p, 3)
            for j in range(4):
                act.wait_ge(sem("conv_val"), j + 1)
                act.activation(yT[:, j, :], yT[:, j, :], ACT.Silu, scale=vec("ln_g", j), bias=vec("ln_b", j))\
                    .then_inc(sem("conv_silu"), 1)
            for j in range(4):
                act.wait_ge(sem("conv_silu"), j + 1)
                act.activation(aH[:, j, :], yT[:, j, :], ACT.Copy).then_inc(sem("conv_hi"), 1)
            n4 = 6 * KD + 4
            gemm(PH["out2c"], lambda it, t: square(n4 + t, lambda: xT[:, bass.ds(it * 4 + t, 1), :].rearrange("p o s -> p (o s)"), it,
                                                   (sem("bank_free"), it * 4 + (NBANK + PH["out2c"].t0 + t + 1))))
            act.preload_act_table_set("natural_log_exp_and_others")
            high_of_x("h4", "g_norm2")
            swiglu(PH["gu2"], "ff2", 8)
            p = PH["dn2"]

            def token_major(kts):
                for kt in kts:
                    if kt % 2 == 0:
                        act.wait_ge(sem("outT"), OUT_ORDER.index(kt) + 1)
                        act.activation(os_[:, :, kt * P:(kt + 1) * P], B[OUT_BANK[kt]][:].rearrange("p (t d) -> p t d", t=TT),
                                       ACT.Copy).then_inc(sem("out_even"), 1)
            with act.Fori(0, 1) as it:
                for j in range(p.nc4):
                    ahead(p, j, it)
            for t in range(4):
                for q in range(3):
                    ahead(p, 3 * t + q, 1, True)
                token_major(OUT_AFTER[t])
            token_major(OUT_AFTER[4])

        @block.tensor
        def _(pe):
            def tile_products(p, it, base, tiles, H, L, first=None, mid=None):
                for t in range(tiles):
                    if mid is not None and t == 2:
                        mid()
                    pe.wait_ge(sem("bank_free"), it * 4 + (p.t0 + base + t + 1))
                    bank = B[(p.t0 + base + t) % NBANK]
                    for k in range(p.k):
                        q, b = p.chunk_of(t, k)
                        q += base * p.nc4 // 4
                        s = (p.c0 + q) % 2
                        if b == 0:
                            pe.wait_ge(sem("w_lo"), it * p.nc4 + (p.c0 + q + 1))
                        if first is not None and t == 0:
                            pe.wait_ge(sem(first), k + 1)
                        hi, lo = wH[:, s, b * P:(b + 1) * P], wL[:, s, b * P:(b + 1) * P]
                        pe.matmul(bank[:], hi, H[:, k, :], start=(k == 0), stop=False)
                        pe.matmul(bank[:], hi, L[:, k, :], start=False, stop=False)
                        mm = pe.matmul(bank[:], lo, H[:, k, :], start=False, stop=(k == p.k - 1))
                        if b == CB - 1 or k == p.k - 1 and p.k != CB // 2:
                            mm.then_inc(sem("chunk_done"), 1)

            def gemm(p, H=aH, L=aL, first=None, mid=None):
                n4 = p.nt // 4
                if first is not None:
                    tile_products(p, 0, 0, 4, H, L, first, mid)
                with pe.Fori(0 if first is None else 1, n4) as it:
                    tile_products(p, it, 0, 4, H, L)
                if p.nt % 4:
                    tile_products(p, 0, n4 * 4, p.nt % 4, H, L)

            def beside(p, it, per, banks, units, ago):
                for u in units:
                    t, k = u // KD, u % KD
                    bank = B[banks[t % len(banks)]]
                    s = (p.c0 + t) % 2
                    if k == 0:
                        pe.wait_ge(sem("bank_free"), it * per + (NBANK + p.t0 + t - ago))
                        pe.wait_ge(sem("w_lo"), it * per + (p.c0 + t + 1))
                    hi, lo = wH[:, s, k * P:(k + 1) * P], wL[:, s, k * P:(k + 1) * P]
                    pe.matmul(bank[:], hi, aH[:, k, :], start=(k == 0), stop=False)
                    pe.matmul(bank[:], hi, aL[:, k, :], start=False, stop=False)
                    mm = pe.matmul(bank[:], lo, aH[:, k, :], start=False, stop=(k == KD - 1))
                    if k == KD - 1:
                        mm.then_inc(sem("chunk_done"), 1)

            def total(used, bank):
                pe.wait_ge(sem("sq_used"), used)
                pe.matmul(bank[:], ones, ssum[:], start=True, stop=True).then_inc(sem("sum_ready"), 1)

            pe.wait_ge(sem("ones_landed"), 16)
            for t in range(TT):
                pe.wait_ge(sem(f"x_landed{t}"), 16)
                for kt in range(KD):
                    mm = pe.transpose(B[kt][:, t * P:(t + 1) * P], xs[:, t, kt * P:(kt + 1) * P], ident)
                    if t == TT - 1:
                        mm.then_inc(sem("xT_psum"), 1)
            p = PH["in1"]

            def group(g, tiles=4, **kw):
                tile_products(p, 0, 4 * g, tiles, aH, aL, **kw)
            group(0, first="h1_lo", mid=lambda: total(KD, B[4]))
            with pe.Fori(1, 3) as it:
                tile_products(p, it, 0, 4, aH, aL)

            pe.wait_ge(sem("ct_landed"), 16)
            pe.wait_ge(sem("bank_free"), NBANK + p.t0 + 8)
            for tile, bank, name in ((VST, B[4], "v_T"), (VWT, B[5], "v_T"), (MISC, B[6], "gate_T")):
                for t in range(TT):
                    mm = pe.transpose(bank[:, t * P:(t + 1) * P], pj[:, tile, t * P:(t + 1) * P], ident)
                mm.then_inc(sem(name), 1)
            group(3)
            pe.wait_ge(sem("small_landed"), 16 * 9)
            pe.wait_ge(sem("kin_ready"), 4)
            for i, w1 in enumerate((w1k, w1v)):
                for l in range(CL):
                    for g in range(NG):
                        r = slice(g * DH, (g + 1) * DH)
                        mm = pe.matmul(B[7][r, i * 64:i * 64 + NCMP], w1[r, l, :], kin[i][r, l, :],
                                       start=(l == 0), stop=(l == CL - 1))
            mm.then_inc(sem("cmp_hid"), 1)

            def log_gate(h):
                pe.matmul(B[ALPHA_BANK[h]][:], wa2[:, h * DK:(h + 1) * DK], pj[0:RANK, MISC, :], start=True, stop=True)\
                    .then_inc(sem("alpha_z"), 1)
            pe.wait_ge(sem("v_S"), 2)
            log_gate(0)
            log_gate(1)
            group(4)
            pe.wait_ge(sem("hid_ready"), 2)
            pe.wait_ge(sem("gates_ready"), 1)
            pe.wait_ge(sem("b_ready"), 2)
            for g in range(NG):
                r = slice(g * DH, (g + 1) * DH)
                pe.matmul(B[6][r, 0:NCMP], w2k[r, :], hid[r, 0, :], start=True, stop=True)
                mm = pe.matmul(B[(7, 5)[g]][0:NCMP, 0:DH], hid[r, 1, :], w2v[r, :], start=True, stop=True)
            mm.then_inc(sem("cmp_kv"), 1)
            group(5)
            log_gate(2)
            pe.wait_ge(sem("cmp_out"), 1 + NG)
            log_gate(3)
            group(6, 3)
            pe.wait_ge(sem("bank_free"), NBANK + PH["r"].t0)
            pe.wait_ge(sem("b_ready"), GH)

            pe.wait_ge(sem("attn_zero"), 1)
            with pe.Fori(0, GH) as h:
                pe.wait_ge(sem("gla_head"), h + 1)
                pe.wait_ge(sem("gla_v"), h + 1)
                for t in range(TT):
                    for e in range(2):
                        mm = pe.transpose(B[t // 2][:, (t % 2) * DV + e * P:(t % 2) * DV + (e + 1) * P],
                                          tmp[:, e, t * P:(t + 1) * P], ident)
                mm.then_inc(sem("gla_vT"), 1)
                at = [0]

                def gate_products():
                    n = R_UNITS[at[0]]
                    first = sum(R_UNITS[:at[0]])
                    beside(PH["r"], h, 2, (3,), range(first, first + n), 0)
                    at[0] += 1
                gate_products()
                pe.wait_ge(sem("gla_qk"), h * 3 + 3)
                for t in range(TT):
                    mm = pe.transpose(B[4][:, t * P:(t + 1) * P], kd[:, t * P:(t + 1) * P], ident)
                mm.then_inc(sem("gla_kdT"), 1)
                for t in range(TT):
                    c = slice(t * P, (t + 1) * P)
                    mm = pe.matmul(B[5][:, c], ke[:, c], qe[:, c], start=True, stop=True)
                mm.then_inc(sem("gla_s"), 1)
                gate_products()
                pe.wait_ge(sem("gla_vS"), h * 2 + 2)
                pe.wait_ge(sem("gla_kdS"), h + 1)
                for c in range(NCH - 1):
                    r = slice((c % 2) * CH, (c % 2) * CH + CH)
                    pe.matmul(upd_bank(c), kdS[r, c // 2, :], vS[r, c // 2, :],
                              start=True, stop=True).then_inc(sem("gla_upd"), 1)
                gate_products()
                pe.wait_ge(sem("gla_att"), h + 1)
                pe.wait_ge(sem("gla_st"), h * (NCH - 1) + (NCH - 1))
                for e in range(2):
                    ec = slice(e * P, (e + 1) * P)
                    for t in range(TT):
                        pe.matmul(B[e][:, t * P:(t + 1) * P], vS[:, t, ec], attnT[:, t, :], start=True, stop=(t == 0),
                                  skip_group_check=True)
                        for c in (2 * t, 2 * t + 1):
                            if c:
                                cc = slice(c * CH, (c + 1) * CH)
                                mm = pe.matmul(B[e][:, cc], st[:, c - 1, ec], qe[:, cc], start=False, stop=True,
                                               skip_group_check=True)
                    mm.then_inc(sem("gla_o"), 1)
                gate_products()
                pe.wait_ge(sem("gla_sq"), h * 2 + 2)
                pe.matmul(B[4][:], ones, sq[:, 0, :], start=True, stop=False)
                pe.matmul(B[4][:], ones, sq[:, 1, :], start=False, stop=True).then_inc(sem("gla_ms"), 1)

            pe.wait_ge(sem("gla_head"), GH + 1)
            kT = (pj[:, KST, :], pj[:, KWT, :])
            vv = (vsS, vwS)
            with pe.Fori(0, NR) as r:
                done = [0]

                def gate_products(n):
                    beside(PH["mgn"], r, 4, MBANK, range(done[0], done[0] + n), 1)
                    done[0] += n
                gate_products(M_START)
                pe.wait_ge(sem("nsa_q"), r + 1)
                pe.wait_ge(sem("nsa_max"), r * NST + 2)
                for g in range(NG):
                    row = slice(g * DH, (g + 1) * DH)
                    for i in range(TT):
                        mm = pe.matmul(B[2 + g][:, i * NCP:(i + 1) * NCP], qst[row, i * P:(i + 1) * P], kcT[row, :],
                                       start=True, stop=True)
                    mm.then_inc(sem("cmp_s"), 1)
                for k in range(NSQ + 2):
                    if k < NST:
                        g, br, i = GROUPS[k]
                        row = slice(g * DH, (g + 1) * DH)
                        if k < NG:
                            pe.wait_ge(sem("cmp_read"), r * NG + k + 1)
                        else:
                            pe.wait_ge(sem("nsa_max"), r * NST + (k + 1))
                        pe.matmul(B[2 + k % 2][:, 0:(i + 1) * P], qst[row, i * P:(i + 1) * P],
                                  kT[br][row, 0:(i + 1) * P], start=True, stop=True).then_inc(sem("nsa_s"), 1)
                        gate_products(M_STEP[i])
                    if 1 <= k <= NST:
                        q = k - 1
                        g, br, i = GROUPS[q]
                        pe.wait_ge(sem("nsa_exp"), r * NST + (q + 1))
                        pe.wait_ge(sem("nsa_pTS"), r * NSQ + (2 if q == 0 else q + 1))
                        for kt in range(i + 1):
                            mm = pe.transpose(B[4 * (q % 2)][:, kt * P:(kt + 1) * P], pS[:, q % 2, kt * P:(kt + 1) * P],
                                              ident)
                        mm.then_inc(sem("nsa_pT"), 1)
                    if k == NSQ:
                        pe.wait_ge(sem("cmp_p"), r + 1)
                        pe.wait_ge(sem("nsa_pTS"), r * NSQ + NSQ)
                        pe.sem_inc(sem("pe_held"), 1)
                        for i in range(TT):
                            mm = pe.transpose(B[0][0:NG * NCP, i * P:(i + 1) * P],
                                              scS[:, i, :, :].rearrange("p g n -> p (g n)"), ident)
                        mm.then_inc(sem("nsa_pT"), 1)
                    if 2 <= k <= NST + 1:
                        q = k - 2
                        g, br, i = GROUPS[q]
                        pe.wait_ge(sem("nsa_pTS"), r * NSQ + (q + 3))
                        for kt in range(i + 1):
                            mm = pe.matmul(B[5 + br][:, i * P + g * DH:i * P + (g + 1) * DH],
                                           pT[:, q % 2, kt * P:(kt + 1) * P], vv[br][:, kt, g * DH:(g + 1) * DH],
                                           start=(kt == 0), stop=(kt == i))
                        mm.then_inc(sem("nsa_pv"), 1)
                pe.wait_ge(sem("nsa_pTS"), r * NSQ + (NST + 3))
                for i in range(TT):
                    mm = pe.matmul(B[3][:, i * P:(i + 1) * P], pT[0:NG * NCP, 0, i * P:(i + 1) * P], vcS[:],
                                   start=True, stop=True)
                mm.then_inc(sem("nsa_pv"), 1)
                gate_products(M_END)
                pe.wait_ge(sem("nsa_acc"), r + 1)
                for i in range(TT):
                    mm = pe.transpose(B[4][:, i * P:(i + 1) * P], oacc[:, i, :], ident)
                mm.then_inc(sem("nsa_oT"), 1)

            pe.wait_ge(sem("nsa_out"), NR)
            pe.wait_ge(sem("bank_free"), NBANK + PH["pg"].t0)
            gemm(PH["pg"], first="og_lo")
            pe.wait_ge(sem("on_lo"), KD // 2)
            gemm(PH["pn"], onH, onL)
            gemm(PH["out1"], first="mix1_lo")
            total(2 * KD, B[4])
            gemm(PH["gu1"], first="h2_lo", mid=lambda: total(3 * KD, B[5]))
            pe.wait_ge(sem("ff1_fL"), KF + 2)
            gemm(PH["dn1"], fH, fL)
            total(4 * KD, B[4])
            p = PH["in2"]
            tile_products(p, 0, 0, 4, aH, aL, "h3_lo", lambda: total(5 * KD, B[5]))
            with pe.Fori(1, 2) as it:
                tile_products(p, it, 0, 4, aH, aL)

            def head_sums(j):
                pe.wait_ge(sem("sq_ready"), 5 * KD + j + 1)
                pe.matmul(B[4][0:NACH, :], cst("sel")[:, j * NACH:(j + 1) * NACH], sq[:, j % 2, :], start=(j == 0),
                          stop=(j == KD - 1), skip_group_check=True).then_inc(sem("sq_used"), 1)

            def head_roots(n, j):
                if n == 0:
                    pe.wait_ge(sem("qk_root"), 1)
                if n >= 2:
                    pe.wait_ge(sem("qk_normed"), n - 1)
                pe.matmul(B[4 + n % 2][:], spread[:, j * P:(j + 1) * P], ssum[0:NACH, :], start=True, stop=True)\
                    .then_inc(sem("qk_spread"), 1)

            def values(j):
                pe.wait_ge(sem("na_vst"), TT * (j + 1))
                if j:
                    pe.wait_ge(sem("na_VS"), 2 * j)
                for i in range(TT):
                    for v in range(2):
                        mm = pe.transpose(B[6 + i // 2][:, (i % 2 * 2 + v) * P:(i % 2 * 2 + v + 1) * P],
                                          vst[:, i, v * P:(v + 1) * P], ident)
                mm.then_inc(sem("na_VT"), 1)

            for t in range(8, 20, 4):
                for u in range(4):
                    tile_products(p, 0, t + u, 1, aH, aL)
                    if 8 < t + u <= 16:
                        head_sums(t + u - 9)
                    if t + u > 16 and t + u < 19:
                        values(t + u - 17)
            pe.wait_ge(sem("spread_landed"), 16)
            for j in range(4):
                head_roots(2 * j, j)
                head_roots(2 * j + 1, 4 + j)
                if j % 2:
                    values(2 + j // 2)
            pe.wait_ge(sem("bank_free"), NBANK + PH["out2n"].t0)
            pe.wait_ge(sem("qk_normed"), 8)
            pe.wait_ge(sem("na_VS"), 8)
            kg = k2[:].rearrange("p a (r c) -> p a r c", r=GR)
            with pe.Fori(0, 2) as it:
                def back(pp):
                    pe.wait_ge(sem("na_norm"), it * 2 + pp + 1 + 1)
                    pe.wait_ge(sem("na_pair"), it * 2 + pp + 1)
                    for i in range(TT):
                        mm = pe.transpose(B[0][:, i * P:(i + 1) * P], o2[:, i, :], ident)
                    mm.then_inc(sem("na_oT"), 1)
                for m in range(NS2 + 3):
                    if m < NS2:
                        pp, hf, i = STEPS2[m]
                        row = slice(hf * DH, (hf + 1) * DH)
                        if m % 8 == 0:
                            pe.wait_ge(sem("na_qk"), it * 4 + 2 * pp + 2)
                        pe.wait_ge(sem("na_max"), it * NS2 + max(0, m - 2) + 1)
                        pe.matmul(B[1 + m % 3][:, 0:GR * KC], q2[row, pp, i * P:(i + 1) * P],
                                  kg[row, pp, :, KEY_BASE[i]:KEY_BASE[i] + KC], start=True, stop=True)\
                            .then_inc(sem("na_s"), 1)
                    if 2 <= m < NS2 + 2:
                        q = m - 2
                        pe.wait_ge(sem("na_exp"), it * NS2 + (q + 1) + 1)
                        pe.wait_ge(sem("na_pTS"), it * NS2 + max(0, q - 1) + 1)
                        for v in range(2):
                            mm = pe.transpose(B[4 + q % 2][:, v * P:(v + 1) * P], p2[:, q % 3, v * P:(v + 1) * P], ident)
                        mm.then_inc(sem("na_pT"), 1)
                    if m >= 3:
                        q = m - 3
                        pp, hf, i = STEPS2[q]
                        if q % 8 == 0:
                            pe.wait_ge(sem("na_norm"), it * 2 + 1)
                        pe.wait_ge(sem("na_pTS"), it * NS2 + (q + 1) + 1)
                        for v in range(2):
                            mm = pe.matmul(B[6 + pp][:, i * P + hf * DH:i * P + (hf + 1) * DH],
                                           pT2[:, q % 2, v * P:(v + 1) * P],
                                           VS[:, i, v, bass.ds(it * (2 * P) + (pp * P + hf * DH), DH)],
                                           start=(v == 0), stop=(v == 1))
                        mm.then_inc(sem("na_pv"), 1)
                    if m == 13:
                        back(0)
                back(1)
            pe.wait_ge(sem("na_pair"), NH // 2 + 1)
            p = PH["out2n"]

            def total_channels():
                pe.wait_ge(sem("ln_add"), 3)
                pe.matmul(B[4][:], ones, ssum[:], start=True, stop=True).then_inc(sem("sum_ready"), 1)
            tile_products(p, 0, 0, 4, aH[:, KD // 2:], aL[:, KD // 2:], None, total_channels)
            tile_products(p, 0, 4, 4, aH[:, KD // 2:], aL[:, KD // 2:], None, lambda: total(6 * KD + 4, B[5]))
            gemm(PH["out2c"], first="conv_lo")
            gemm(PH["gu2"], first="h4_lo", mid=lambda: total(7 * KD + 4, B[4]))
            pe.wait_ge(sem("ff2_fL"), KF + 2)
            p = PH["dn2"]
            with pe.Fori(0, 1) as it:
                tile_products(p, it, 0, 4, fH, fL)

            def token_major(kts):
                for kt in kts:
                    n = OUT_ORDER.index(kt)
                    pe.wait_ge(sem("bank_free"), NBANK + p.t0 + kt + 1)
                    if n >= 4:
                        before = OUT_ORDER[n - 4]
                        pe.wait_ge(sem("out_odd" if before % 2 else "out_even"), before // 2 + 1)
                    for t in range(TT):
                        mm = pe.transpose(B[OUT_BANK[kt]][:, t * P:(t + 1) * P], xT[:, kt, t * P:(t + 1) * P], ident)
                    mm.then_inc(sem("outT"), 1)
            for t in range(4):
                tile_products(p, 0, 4 + t, 1, fH, fL)
                token_major(OUT_AFTER[t])
            token_major(OUT_AFTER[4])

        @block.vector
        def _(dve):
            chain = [0]

            def link(ins):
                chain[0] += 1
                ins.then_inc(sem("dve_link"), 1)
                dve.wait_ge(sem("dve_link"), chain[0])

            dve.memset(nr[:, 0:1], 0.0).then_inc(sem("bank_free"), NBANK)
            for name, n in (("gla_head", 1), ("nsa_max", 2), ("nsa_pT", 2), ("nsa_pTS", 2),
                            ("conv_add", 2), ("ff1_fL", 2), ("ff2_fL", 2)):
                dve.sem_inc(sem(name), n)
            for name in ("na_max", "na_exp", "na_pT", "na_pTS", "na_pv", "na_norm", "na_pair", "na_oT"):
                dve.sem_inc(sem(name), 1)

            def newton(n, rows=P, r=nr):
                r, x, t = r[0:rows, :], nx[0:rows, :], nt_[0:rows, :]
                dve.wait_ge(sem("nr_ready"), n)
                link(dve.scalar_tensor_tensor(t, r, -0.5, r, ALU.mult, ALU.mult))
                link(dve.tensor_tensor(t, t, x, ALU.mult))
                link(dve.scalar_tensor_tensor(r, t, 1.5, r, ALU.add, ALU.mult))

            def clear_sum(n):
                if n:
                    dve.wait_ge(sem("sum_ready"), n)
                link(dve.memset(ssum[:], 0.0))

            def add_square(n, it=0):
                dve.wait_ge(sem("sq_ready"), it * 4 + (n + 1))
                dve.wait_ge(sem("sq_used"), it * 4 + n)
                dve.tensor_tensor(ssum[:], ssum[:], sq[:, n % 2, :], ALU.add).then_inc(sem("sq_used"), 1)

            def norm(sums, n, bank):
                dve.wait_ge(sem("sum_ready"), sums)
                dve.tensor_scalar(nx[:], bank[:], 1.0 / D, EPS, ALU.mult, ALU.add).then_inc(sem("nx_ready"), 1)
                newton(n)

            def low_of_x(use, gain, kt):
                dve.wait_ge(sem(use + "_hi"), kt + 1)
                dve.scalar_tensor_tensor(aL[:, kt, :], xT[:, kt, :], vec(gain, kt), aH[:, kt, :].bitcast(F32),
                                         ALU.mult, ALU.subtract).then_inc(sem(use + "_lo"), 1)

            def low_of(use, src, n):
                for kt in range(n):
                    dve.wait_ge(sem(use + "_hi"), kt + 1)
                    dve.tensor_tensor(aL[:, kt, :], src(kt), aH[:, kt, :].bitcast(F32), ALU.subtract)\
                        .then_inc(sem(use + "_lo"), 1)

            def evict(p, write, groups=None):
                def body(it, base, tiles):
                    for t in range(tiles):
                        dve.wait_ge(sem("chunk_done"), it * p.nc4 + (p.c0 + base * p.nc4 // 4 + p.last_chunk(t)))
                        write(it, base + t, B[(p.t0 + base + t) % NBANK])
                n4 = p.nt // 4 if groups is None else groups
                with dve.Fori(0, n4) as it:
                    body(it, 0, 4)
                if groups is None and p.nt % 4:
                    body(0, n4 * 4, p.nt % 4)

            def normed_to(dst):
                def write(it, t, bank):
                    dve.tensor_tensor(dst[:, bass.ds(it * 4 + t, 1), :], bank[:].unsqueeze(1), nr[:].unsqueeze(1), ALU.mult)\
                        .then_inc(sem("bank_free"), 1)
                return write

            def copy_and_square(dst, u):
                def write(it, t, bank):
                    dve.tensor_scalar(dst[:, bass.ds(it * 4 + t, 1), :], bank[:], 1.0, None, ALU.mult).then_inc(sem("bank_free"), 1)
                    add_square(u * KD + t, it)
                return write

            dve.wait_ge(sem("pv_landed"), 16)
            for kt in range(KD):
                dve.wait_ge(sem("xT_psum"), kt + 1)
                dve.tensor_copy(xT[:, kt, :], B[kt][:]).then_inc(sem("xT_ready"), 1)
                if kt:
                    low_of_x("h1", "g_mix_pre", kt - 1)
            low_of_x("h1", "g_mix_pre", KD - 1)
            clear_sum(0)
            for kt in range(KD):
                add_square(kt)
            norm(1, 1, B[4])
            p = PH["in1"]

            def group(g, tiles=4):
                for t in range(4 * g, 4 * g + tiles):
                    dve.wait_ge(sem("chunk_done"), p.c0 + t + 1)
                    slot = t + IN1_FIRST if t < IN1_EARLY else t - IN1_EARLY
                    dve.tensor_tensor(pj[:, slot, :], B[(p.t0 + t) % NBANK][:], nr[:], ALU.mult)\
                        .then_inc(sem("bank_free"), 1)
            with dve.Fori(0, 2) as it:
                for t in range(4):
                    dve.wait_ge(sem("chunk_done"), it * 4 + (p.c0 + t + 1))
                    dve.tensor_tensor(pj[:, bass.ds(it * 4 + (IN1_FIRST + t), 1), :], B[(p.t0 + t) % NBANK][:].unsqueeze(1),
                                      nr[:].unsqueeze(1), ALU.mult).then_inc(sem("bank_free"), 1)
            dve.wait_ge(sem("bank_free"), NBANK + p.t0 + 8)
            for i, (tile, pe_name) in enumerate(((KCT, "pe_k"), (VCT, "pe_v"))):
                for a in range(CL // CST):
                    src = pj[:, tile, a * CST:a * CST + NCMP * CST].rearrange("p (n b) -> p b n", b=CST)
                    pos = pv[:, PV_AT[pe_name] + a * CST:PV_AT[pe_name] + (a + 1) * CST].unsqueeze(2)\
                        .to_broadcast([P, CST, NCMP])
                    dve.tensor_tensor(kin[i][:, a * CST:(a + 1) * CST, :], src, pos, ALU.add).then_inc(sem("kin_ready"), 1)
            group(2)
            dve.wait_ge(sem("v_T"), 2)
            dve.tensor_copy(vsS[:], B[4][:].rearrange("p (t c) -> p t c", t=TT)).then_inc(sem("v_S"), 1)
            dve.tensor_copy(vwS[:], B[5][:].rearrange("p (t c) -> p t c", t=TT)).then_inc(sem("v_S"), 1)
            group(3)

            dve.wait_ge(sem("ct_landed"), 16)

            def log_gate(h):
                dve.wait_ge(sem("la_act"), 3 * h + 3)
                link(dve.tensor_scalar(bT[:, h, :], B[ALPHA_BANK[h]][:], vec("b_alpha", h), 0.0, ALU.add, ALU.min))
                link(dve.tensor_tensor(bT[:, h, :], bT[:, h, :], tmp[:, h % 2, :], ALU.subtract))
                dve.tensor_tensor_scan(bT[:, h, :], cst("reset"), bT[:, h, :], 0.0, ALU.mult, ALU.add)\
                    .then_inc(sem("b_ready"), 1)
            log_gate(0)
            log_gate(1)
            dve.memset(attnT[:], 0.0).then_inc(sem("attn_zero"), 1)
            group(4)
            link(dve.memset(kcT[:], 0.0))
            link(dve.memset(vcS[:], 0.0))
            dve.wait_ge(sem("cmp_kv"), 1)
            dve.tensor_copy(kcT[:, 0:NCMP], B[6][:, 0:NCMP]).then_inc(sem("cmp_out"), 1)
            for g in range(NG):
                dve.tensor_copy(vcS[g * NCP:g * NCP + NCMP, g * DH:(g + 1) * DH], B[(7, 5)[g]][0:NCMP, 0:DH])\
                    .then_inc(sem("cmp_out"), 1)
            group(5)
            log_gate(2)
            log_gate(3)
            group(6, 3)
            dve.wait_ge(sem("bank_free"), NBANK + PH["r"].t0)
            dve.wait_ge(sem("b_ready"), GH)
            dve.wait_ge(sem("attn_zero"), 1)

            def beside(p, it, per, t, bank, first):
                dve.wait_ge(sem("chunk_done"), it * per + (p.c0 + t + 1))
                dve.tensor_tensor(pj[:, bass.ds(it * per + (first + t), 1), :], bank[:].unsqueeze(1), nr[:].unsqueeze(1), ALU.mult)\
                    .then_inc(sem("bank_free"), 1)

            def gate_tile(h, t):
                beside(PH["r"], h, 2, t, B[3], GRR)

            with dve.Fori(0, GH) as h:
                bh = bT[:, bass.ds(h, 1), :].rearrange("p o (n c) -> p (o n) c", c=CH)
                dve.tensor_tensor(kd[:].rearrange("p (n c) -> p n c", c=CH),
                                  bh[:, :, CH - 1:CH].to_broadcast([P, NCH, CH]), bh, ALU.subtract)\
                    .then_inc(sem("gla_dif"), 1)
                dve.wait_ge(sem("gla_exp"), h * 4 + 3)
                dve.scalar_tensor_tensor(qe[:], pj[:, bass.ds(h + GQ, 1), :], DK ** -0.5, qe[:], ALU.mult, ALU.mult)\
                    .then_inc(sem("gla_qk"), 1)
                dve.tensor_tensor(ke[:], pj[:, bass.ds(h + GK, 1), :], ke[:], ALU.mult).then_inc(sem("gla_qk"), 1)
                dve.wait_ge(sem("gla_exp"), h * 4 + 4)
                dve.tensor_tensor(kd[:], pj[:, bass.ds(h + GK, 1), :], kd[:], ALU.mult).then_inc(sem("gla_qk"), 1)
                dve.wait_ge(sem("gla_s"), h + 1)
                dve.sem_inc(sem("dve_held"), 1)
                dve.copy_predicated(attnT[:], cst("causal64").bitcast(I32).unsqueeze(1).to_broadcast([P, TT, P]),
                                    B[5][:].rearrange("p (t c) -> p t c", t=TT)).then_inc(sem("gla_att"), 1)
                gate_tile(h, 0)
                for c in range(NCH - 1):
                    u = upd_bank(c)
                    dve.wait_ge(sem("gla_upd"), h * (NCH - 1) + min(NCH - 1, 4 * (c // 4) + 3 + c % 2))
                    if c == 0:
                        dve.tensor_copy(st[:, 0, :], u).then_inc(sem("gla_st"), 1)
                    else:
                        dve.wait_ge(sem("gla_st"), h * (NCH - 1) + c)
                        dve.scalar_tensor_tensor(st[:, c, :], st[:, c - 1, :], dec[:, c:c + 1], u, ALU.mult, ALU.add)\
                            .then_inc(sem("gla_st"), 1)
                dve.wait_ge(sem("gla_sq"), h * 2 + 2)
                dve.wait_ge(sem("gla_qk"), h * 3 + 3)
                dve.tensor_scalar(pj[:, bass.ds(h + GQ, 1), :], B[0][:].unsqueeze(1), vec("gla_g", 0), None, ALU.mult)
                dve.tensor_scalar(pj[:, bass.ds(h + GK, 1), :], B[1][:].unsqueeze(1), vec("gla_g", 1), None, ALU.mult).then_inc(sem("gla_raw"), 1)
                gate_tile(h, 1)
                dve.wait_ge(sem("gla_ms"), h + 1)
                dve.tensor_scalar(bT[:, bass.ds(h, 1), :], B[4][:], 1.0 / DV, EPS, ALU.mult, ALU.add)\
                    .then_inc(sem("gla_head"), 1)
            dve.wait_ge(sem("gla_head"), GH + 1)

            dve.wait_ge(sem("gates_ready"), 1)
            gview = gates[:].rearrange("p i (g r b) -> p r b i g", g=NG, r=NR)
            with dve.Fori(0, NR) as r:
                for g in range(NG):
                    dve.wait_ge(sem("cmp_s"), r * NG + g + 1)
                    dve.tensor_tensor(scS[:, :, g, :], B[2 + g][:, 0:TT * NCP].rearrange("p (i n) -> p i n", n=NCP),
                                      biasc[:, :, g, :], ALU.add).then_inc(sem("cmp_read"), 1)
                for k in range(NSQ + 1):
                    if k < NST:
                        g, br, i = GROUPS[k]
                        n = (i + 1) * P
                        dve.wait_ge(sem("nsa_s"), r * NST + (k + 1))
                        if k >= 2:
                            dve.wait_ge(sem("nsa_exp"), r * NST + (k - 1))
                        dve.sem_inc(sem("dve_held"), 1)
                        dve.tensor_tensor_reduce(out=sS[:, k % 2, 0:n], in0=B[2 + k % 2][:, 0:n], in1=biasg[g][:, S - n:S],
                                                 scale=-1.0, scalar=3e38, op0=ALU.add, op1=ALU.min,
                                                 accum_out=nmx[:, k:k + 1]).then_inc(sem("nsa_max"), 1)
                    if k == 0:
                        dve.wait_ge(sem("cmp_read"), r * NG + NG)
                        dve.tensor_reduce(cmx[:], scS[:], AX.X, ALU.max).then_inc(sem("cmp_dve"), 1)
                        dve.wait_ge(sem("cmp_dve"), r * 2 + 1)
                        dve.tensor_tensor(scS[:], scS[:], cmx[:].unsqueeze(3).to_broadcast([P, TT, NG, NCP]), ALU.subtract)\
                            .then_inc(sem("cmp_sub"), 1)
                    if k == 2:
                        dve.wait_ge(sem("cmp_exp"), r + 1)
                        dve.tensor_reduce(rsum[:, 2], scS[:], AX.X, ALU.add).then_inc(sem("cmp_dve"), 1)
                        dve.wait_ge(sem("cmp_dve"), r * 2 + 2)
                        dve.tensor_tensor(scS[:], scS[:], maskc, ALU.mult).then_inc(sem("cmp_p"), 1)
                    if k in M_OUT:
                        beside(PH["mgn"], r, 4, M_OUT.index(k), B[MBANK[M_OUT.index(k) % 2]], 0)
                    if k == NST:
                        dve.wait_ge(sem("nsa_max"), r * NST + (NST + 2))
                        dve.tensor_scalar(biasg[0], biasg[0], 0.5, None, ALU.mult)
                        dve.tensor_scalar(biasg[1], biasg[1], 0.5, None, ALU.mult)
                        dve.tensor_scalar(biasc, biasc, 0.5, None, ALU.mult).then_inc(sem("bias_half"), 1)
                        dve.wait_ge(sem("nsa_exp"), r * NST + NST)
                        dve.reciprocal(gsc[:], rsum[:]).then_inc(sem("nsa_dve"), 1)
                        dve.wait_ge(sem("nsa_dve"), r * 8 + 1)
                        for j, b in enumerate((1, 2, 0)):
                            dve.tensor_tensor(gsc[:, j], gsc[:, j], gview[:, bass.ds(r, 1), b].rearrange("p o i g -> p (o i) g"),
                                              ALU.mult).then_inc(sem("nsa_dve"), 1)
                    if k >= 1:
                        q = k - 1
                        n, rows = ((GROUPS[q][2] + 1) * P, P) if q < NST else (S, NG * NCP)
                        dve.wait_ge(sem("nsa_pT"), r * NSQ + (q + 3))
                        if q >= 2:
                            dve.wait_ge(sem("nsa_pv"), r * NSQ + (q - 1))
                        dve.tensor_copy(pT[0:rows, q % 2, 0:n], B[4 * (q % 2)][0:rows, 0:n]).then_inc(sem("nsa_pTS"), 1)
                dve.wait_ge(sem("nsa_dve"), r * 8 + 4)
                dve.wait_ge(sem("bias_half"), r + 1)
                oav = oacc[:].rearrange("p i (g d) -> p (i g) d", g=NG)
                otv = otmp[:].rearrange("p i (g d) -> p (i g) d", g=NG)

                def gated(j, dst):
                    return dve.tensor_tensor(dst, B[(5, 6, 3)[j]][:].rearrange("p (a d) -> p a d", d=DH),
                                             gsc[:, j].rearrange("p i g -> p (i g)").unsqueeze(2).to_broadcast([P, TT * NG, DH]),
                                             ALU.mult).then_inc(sem("nsa_dve"), 1)
                dve.wait_ge(sem("nsa_pv"), r * NSQ + NST)
                gated(0, oav)
                gated(1, otv)
                dve.wait_ge(sem("nsa_dve"), r * 8 + 6)
                dve.tensor_tensor(oav, oav, otv, ALU.add).then_inc(sem("nsa_dve"), 1)
                dve.wait_ge(sem("nsa_dve"), r * 8 + 7)
                dve.wait_ge(sem("nsa_pv"), r * NSQ + NSQ)
                gated(2, otv)
                dve.wait_ge(sem("nsa_dve"), r * 8 + 8)
                dve.tensor_tensor(oav, oav, otv, ALU.add).then_inc(sem("nsa_acc"), 1)
                dve.wait_ge(sem("gla_fin"), 2 * GH)
                beside(PH["mgn"], r, 4, 3, B[MBANK[1]], 0)

            low_of("og", lambda kt: pj[:, GRR + kt, :], KD)
            dve.wait_ge(sem("gates_mix"), 1)

            def times_gate(it, t, bank):
                s_ = sg[:, bass.ds(it * 4 + t, 1), :]
                dve.tensor_tensor(s_, bank[:], s_, ALU.mult).then_inc(sem("bank_free"), 1)
            evict(PH["pg"], times_gate)
            for kt in range(KD // 2):
                dve.wait_ge(sem("on_hi"), kt + 1)
                dve.tensor_tensor(onL[:, kt, :], pj[:, NQ + kt, :], onH[:, kt, :].bitcast(F32), ALU.subtract)\
                    .then_inc(sem("on_lo"), 1)
            dve.wait_ge(sem("gates_mix"), 2)

            def add_gated(it, t, bank):
                dve.wait_ge(sem("bank_free"), it * 4 + (NBANK + PH["pn"].t0 + t - 1))
                dve.tensor_tensor(tmp[:, t % 2, :].unsqueeze(1), bank[:].unsqueeze(1), sgn[:, bass.ds(it * 4 + t, 1), :], ALU.mult)\
                    .then_inc(sem("pn_mul"), 1)
                dve.wait_ge(sem("pn_mul"), it * 4 + (t + 1))
                s_ = sg[:, bass.ds(it * 4 + t, 1), :]
                dve.tensor_tensor(s_, s_, tmp[:, t % 2, :].unsqueeze(1), ALU.add).then_inc(sem("bank_free"), 1)
                dve.wait_ge(sem("mix1_hi"), it * 4 + (t + 1))
                dve.tensor_tensor(aL[:, bass.ds(it * 4 + t, 1), :], s_, aH[:, bass.ds(it * 4 + t, 1), :].bitcast(F32),
                                  ALU.subtract).then_inc(sem("mix1_lo"), 1)
            dve.wait_ge(sem("bank_free"), NBANK + PH["pn"].t0)
            evict(PH["pn"], add_gated)
            clear_sum(1)
            evict(PH["out1"], copy_and_square(zT, 1))

            def residual_and_low(src, gain, name, use, next_gain):
                for kt in range(KD):
                    if kt >= 2:
                        dve.wait_ge(sem(name), kt - 1)
                    dve.scalar_tensor_tensor(tmp[:, kt % 2, :], src[:, kt, :], vec(gain, kt), nr[:], ALU.mult, ALU.mult)\
                        .then_inc(sem(name + "_mul"), 1)
                    if kt >= 2:
                        low_of_x(use, next_gain, kt - 2)
                low_of_x(use, next_gain, KD - 2)
                low_of_x(use, next_gain, KD - 1)

            norm(2, 2, B[4])
            clear_sum(2)
            residual_and_low(zT, "g_mix_post", "res1", "h2", "g_ffn_pre")
            for kt in range(KD):
                add_square(2 * KD + kt)
            norm(3, 3, B[5])

            def swiglu(p, tag):
                with dve.Fori(0, p.nt // 4) as it:
                    for j in range(2):
                        dve.wait_ge(sem("chunk_done"), it * 4 + (p.c0 + 2 * j + 1))
                        dve.wait_ge(sem(tag + "_fL"), it * 2 + (j + 1))
                        dve.tensor_tensor(sq[:, j, :], B[(p.t0 + 2 * j) % NBANK][:], nr[:], ALU.mult)\
                            .then_inc(sem("bank_free"), 1)
                        dve.wait_ge(sem("bank_free"), it * 4 + (NBANK + p.t0 + 2 * j + 1))
                        dve.sem_inc(sem(tag + "_gate"), 1)
                        dve.wait_ge(sem("chunk_done"), it * 4 + (p.c0 + 2 * j + 2))
                        dve.tensor_tensor(tmp[:, j, :], B[(p.t0 + 2 * j + 1) % NBANK][:], nr[:], ALU.mult)\
                            .then_inc(sem("bank_free"), 1)
                        dve.wait_ge(sem("bank_free"), it * 4 + (NBANK + p.t0 + 2 * j + 2))
                        dve.wait_ge(sem(tag + "_silu"), it * 2 + (j + 1))
                        dve.tensor_tensor(tmp[:, j, :], tmp[:, j, :], sq[:, j, :], ALU.mult).then_inc(sem(tag + "_f"), 1)
                        dve.wait_ge(sem(tag + "_fH"), it * 2 + (j + 1))
                        dve.tensor_tensor(fL[:, bass.ds(it * 2 + j, 1), :], tmp[:, j, :].unsqueeze(1),
                                          fH[:, bass.ds(it * 2 + j, 1), :].bitcast(F32), ALU.subtract)\
                            .then_inc(sem(tag + "_fL"), 1)

            swiglu(PH["gu1"], "ff1")
            clear_sum(3)
            evict(PH["dn1"], copy_and_square(z2T, 3))
            norm(4, 4, B[4])
            clear_sum(4)
            residual_and_low(z2T, "g_ffn_post", "res2", "h3", "g_norm1")
            for kt in range(KD):
                add_square(4 * KD + kt)
            dve.wait_ge(sem("res2"), KD)
            dve.sem_inc(sem("ffn1_done"), 1)
            norm(5, 5, B[5])

            evict(PH["in2"], normed_to(pk), 2)
            dve.wait_ge(sem("up_zero"), 1)
            for j in range(4):
                dve.wait_ge(sem("glu_sig"), j + 1)
                dve.tensor_tensor(up[:, j, HP:HP + S], pk[:, j, :], pk[:, 4 + j, :], ALU.mult).then_inc(sem("conv_in"), 1)
            dve.wait_ge(sem("conv_in"), 4)
            for j in range(3):
                w = PV_AT["dw"] + j * TAPS
                dve.tensor_scalar(yT[:, j, :], up[:, j, 0:S], pv[:, w:w + 1], vec("dw_bias", j), ALU.mult, ALU.add)\
                    .then_inc(sem("conv_step"), 1)

            def taps(base, t0, n, channels=range(3)):
                for t in range(t0, t0 + n):
                    for c in channels:
                        w = PV_AT["dw"] + c * TAPS
                        dve.wait_ge(sem("conv_step"), base * 3 + (3 * (t - 1) + c + 1))
                        dve.scalar_tensor_tensor(yT[:, c, :], up[:, c, bass.ds(base + t, S)],
                                                 pv[:, bass.ds(base + (w + t), 1)], yT[:, c, :],
                                                 ALU.mult, ALU.add).then_inc(sem("conv_step"), 1)

            p = PH["in2"]

            def out_of_psum(it, t, bank):
                dve.wait_ge(sem("chunk_done"), it * 2 + (p.c0 + t + 1))
                dve.tensor_tensor(pk[:, bass.ds(it * 2 + t, 1), :], bank[:].unsqueeze(1), nr[:].unsqueeze(1), ALU.mult)\
                    .then_inc(sem("bank_free"), 1)
            with dve.Fori(0, 2) as two:
                for j in range(4):
                    dve.wait_ge(sem("chunk_done"), two * 4 + (p.c0 + 8 + j + 1))
                    dve.tensor_tensor(pk[:, bass.ds(two * 4 + (8 + j), 1), :], B[(p.t0 + j) % NBANK][:].unsqueeze(1),
                                      nr[:].unsqueeze(1), ALU.mult).then_inc(sem("bank_free"), 1)
                    taps(two * (4 * TQ), 1 + TQ * j, TQ)
            for j in range(3):
                out_of_psum(0, 16 + j, B[(p.t0 + j) % NBANK])
                taps(0, T_V + TV * j, TV)
            dve.wait_ge(sem("sq_used"), 6 * KD)
            dve.tensor_scalar(nx[0:NACH, :], B[4][0:NACH, :], 1.0 / DH, EPS, ALU.mult, ALU.add).then_inc(sem("nx_ready"), 1)
            newton(6, NACH, ssum)
            dve.sem_inc(sem("qk_root"), 1)
            out_of_psum(0, 19, B[(p.t0 + 3) % NBANK])
            for n in range(8):
                j = n // 2 + 4 * (n % 2)
                dve.wait_ge(sem("qk_spread"), n + 1)
                dve.scalar_tensor_tensor(pk[:, 8 + j, :], pk[:, 8 + j, :], vec("qn_g" if j < 4 else "kn_g"), B[4 + n % 2][:],
                                         ALU.mult, ALU.mult).then_inc(sem("qk_normed"), 1)

            with dve.Fori(0, 2) as it:
                def over_sums(pp):
                    r = slice(8 * pp, 8 * pp + 8)
                    dve.wait_ge(sem("na_exp"), it * NS2 + 8 * pp + 8 + 1)
                    dve.reciprocal(rs2[:, r], rs2[:, r]).then_inc(sem("na_rec"), 1)
                    dve.wait_ge(sem("na_rec"), it * 2 + pp + 1)
                    dve.wait_ge(sem("na_pv"), it * NS2 + 8 * pp + 8 + 1)
                    dve.wait_ge(sem("na_oT"), it * 2 + pp + 1)
                    dve.tensor_tensor(o2.rearrange("p i (f d) -> p f i d", f=2),
                                      B[6 + pp][:].rearrange("p (i f d) -> p f i d", i=TT, f=2),
                                      rs2[:, r].rearrange("p (f i) -> p f i", f=2).unsqueeze(3).to_broadcast([P, 2, TT, DH]),
                                      ALU.mult).then_inc(sem("na_norm"), 1)

                def low_out(pp):
                    dve.wait_ge(sem("na_hi"), it * 2 + pp + 1)
                    out = [a[:, bass.ds(it * 2 + (pp + 4), 1), :] for a in (aL, aH)]
                    lo, hi = out[0], out[1].bitcast(F32)
                    dve.tensor_tensor(lo.rearrange("p o (r i c) -> p (o i) r c", r=GR, i=TT),
                                      B[0][:].rearrange("p (i r c) -> p i r c", i=TT, r=GR),
                                      hi.rearrange("p o (r i c) -> p (o i) r c", r=GR, i=TT),
                                      ALU.subtract).then_inc(sem("na_pair"), 1)
                for m in range(NS2 + 2):
                    if m < NS2:
                        dve.wait_ge(sem("na_s"), it * NS2 + (m + 1))
                        dve.wait_ge(sem("na_bias"), it * NS2 + (m + 1))
                        dve.wait_ge(sem("na_exp"), it * NS2 + max(0, m - 2) + 1)
                        dve.sem_inc(sem("dve_held"), 1)
                        dve.tensor_tensor_reduce(out=s2[:, m % 3, :], in0=B[1 + m % 3][:, 0:GR * KC],
                                                 in1=bm[:, m % 3].rearrange("p r c -> p (r c)"), scale=-1.0, scalar=3e38,
                                                 op0=ALU.add, op1=ALU.min, accum_out=nm2[:, m:m + 1])\
                            .then_inc(sem("na_max"), 1)
                    if m >= 2:
                        q = m - 2
                        dve.wait_ge(sem("na_pT"), it * NS2 + (q + 1) + 1)
                        dve.wait_ge(sem("na_pv"), it * NS2 + max(0, q - 1) + 1)
                        dve.tensor_copy(pT2[:, q % 2, :], B[4 + q % 2][:, 0:GR * KC]).then_inc(sem("na_pTS"), 1)
                    if 2 <= m < 2 + 3 * TN:
                        taps(it * TN, T_N + (m - 2) // 3, 1, [(m - 2) % 3])
                    if m == 11:
                        over_sums(0)
                    if m == 16:
                        low_out(0)
                over_sums(1)
                low_out(1)

            dve.wait_ge(sem("conv_step"), 3 * TAPS)
            dve.wait_ge(sem("conv_add"), TAPS + 1)
            for j in range(1, 4):
                if j > 1:
                    dve.wait_ge(sem("ln_add"), j - 1)
                dve.tensor_tensor(ssum[:], yT[:, 0, :] if j == 1 else ssum[:], yT[:, j, :], ALU.add).then_inc(sem("ln_add"), 1)

            def add_to_x(it, t, bank):
                x_ = xT[:, bass.ds(it * 4 + t, 1), :]
                dve.tensor_tensor(x_, bank[:].unsqueeze(1), x_, ALU.add).then_inc(sem("bank_free"), 1)

            def add_and_square(it, t, bank):
                add_to_x(it, t, bank)
                add_square(6 * KD + 4 + t, it)

            p = PH["out2n"]

            def attention_part(t):
                dve.wait_ge(sem("chunk_done"), p.c0 + t // 2 + 1)
                dve.tensor_tensor(xT[:, t, :], B[(p.t0 + t) % NBANK][:], xT[:, t, :], ALU.add).then_inc(sem("bank_free"), 1)

            attention_part(0)
            attention_part(1)
            dve.wait_ge(sem("sum_ready"), 6)
            for j in range(4):
                dve.scalar_tensor_tensor(yT[:, j, :], B[4][:], -1.0 / S, yT[:, j, :], ALU.mult, ALU.add)\
                    .then_inc(sem("ln_cen"), 1)
            clear_sum(6)
            for j in range(4):
                add_square(6 * KD + j)
                if j in (1, 3):
                    attention_part(2 + j // 2)
            attention_part(4)
            attention_part(5)
            dve.wait_ge(sem("sum_ready"), 7)
            dve.tensor_scalar(nx[:], B[5][:], 1.0 / S, EPS, ALU.mult, ALU.add).then_inc(sem("nx_ready"), 1)
            newton(7)
            dve.wait_ge(sem("ln_cen"), 4)
            for j in range(4):
                dve.tensor_tensor(yT[:, j, :], yT[:, j, :], nr[:], ALU.mult).then_inc(sem("conv_val"), 1)
            attention_part(6)
            attention_part(7)
            low_of("conv", lambda j: yT[:, j, :], 4)
            clear_sum(7)
            dve.wait_ge(sem("bank_free"), NBANK + PH["out2c"].t0)
            evict(PH["out2c"], add_and_square)
            for kt in range(KD):
                low_of_x("h4", "g_norm2", kt)
            norm(8, 8, B[4])
            swiglu(PH["gu2"], "ff2")
            p = PH["dn2"]

            def token_major(kts):
                for kt in kts:
                    if kt % 2:
                        dve.wait_ge(sem("outT"), OUT_ORDER.index(kt) + 1)
                        dve.tensor_copy(os_[:, :, kt * P:(kt + 1) * P], B[OUT_BANK[kt]][:].rearrange("p (t d) -> p t d", t=TT))\
                            .then_inc(sem("out_odd"), 1)
            for t in range(KD):
                dve.wait_ge(sem("chunk_done"), p.c0 + (t // 4) * p.nc4 + p.last_chunk(t % 4))
                dve.tensor_tensor(xT[:, t, :], B[(p.t0 + t) % NBANK][:], xT[:, t, :], ALU.add).then_inc(sem("bank_free"), 1)
                if t >= 4:
                    token_major(OUT_AFTER[t - 4])
            token_major(OUT_AFTER[4])


def lay_out(inputs):
    f = {k: np.asarray(v) for k, v in inputs.items()}
    f = {k: (v[0] if k != "x" else v[0]) for k, v in f.items()}

    def blocks(w):
        k, n = w.shape[0] // P, w.shape[1] // P
        return w.reshape(k, P, n, P).transpose(1, 2, 0, 3).reshape(P, -1)

    w = f["w_in"]
    z = np.zeros((D, P), np.float32)
    gw = 3 * NH
    at = np.cumsum([0, GH * DK, GH * DK, GH * DV, GH * DV, RANK, NH * DH] + 6 * [NG * DH] + [gw, D, D])
    sec = [w[:, at[i]:at[i + 1]] for i in range(len(at) - 1)]
    misc = np.concatenate([sec[4], z[:, :GATE_ROW - RANK], sec[12], z[:, :P - GATE_ROW - gw]], 1)
    nq = sec[5].reshape(D, NG, NR, DH).transpose(0, 2, 1, 3).reshape(D, NH * DH)
    k_c, v_c, k_s, v_s, k_w, v_w = sec[6:12]
    in1 = np.concatenate([sec[2], sec[0], sec[1], misc, k_c, v_c, v_s, v_w, k_s, k_w, nq], 1)
    in1 = np.concatenate([in1[:, IN1_FIRST * P:], in1[:, :IN1_FIRST * P], sec[3]], 1)
    pn = f["w_proj_nsa"].reshape(NG, NR, DH, D).transpose(1, 0, 2, 3).reshape(NH * DH, D)

    def pairs(g, u):
        return np.stack([g.reshape(D, KF, P), u.reshape(D, KF, P)], 2).reshape(D, 2 * FF)

    stream = np.concatenate(
        [blocks(a) for a in (in1, sec[13], sec[14], f["w_proj_gla"], pn, f["w_out"],
                             pairs(f["w_ffn_gate"], f["w_ffn_up"]), f["w_ffn_down"],
                             f["w_in_2"], f["w_out_2"][D // 2:], f["w_out_2"][:D // 2], pairs(f["w_gate_2"], f["w_up_2"]), f["w_down_2"])]
        + [np.zeros((P, CW), np.float32)], 1)
    assert stream.shape[1] == NBLOCK * P + CW

    def cols(v):
        return v.reshape(-1, P).T

    def twice(v):
        return np.concatenate([v, v], 0)

    pvs = {"g_mix_pre": cols(f["norm_mix_pre"]), "g_mix_post": cols(f["norm_mix_post"]),
           "g_ffn_pre": cols(f["norm_ffn_pre"]), "g_ffn_post": cols(f["norm_ffn_post"]),
           "g_norm1": cols(f["norm1_g_2"]), "g_norm2": cols(f["norm2_g_2"]),
           "b_alpha": cols(f["gla_b_alpha"]), "gla_g": cols(f["gla_norm_g"]),
           "dw_bias": cols(f["dw_bias_2"]), "ln_g": cols(f["conv_ln_g_2"]), "ln_b": cols(f["conv_ln_b_2"]),
           "dw": f["dw_kernel_2"].reshape(TAPS, 4, P).transpose(2, 1, 0).reshape(P, 4 * TAPS),
           "qn_g": twice(f["q_norm_g_2"])[:, None], "kn_g": twice(f["k_norm_g_2"])[:, None],
           "pe_k": twice(f["nsa_cmp_pe_k"].T), "pe_v": twice(f["nsa_cmp_pe_v"].T)}
    pvec = np.concatenate([pvs[n] for n, _ in PV_COLS], 1)
    out = {"x": f["x"], "w": stream, "pv": pvec, "ct": constants(), "wa2": f["gla_w_alpha2"],
           "w1k": f["nsa_cmp_w1_k"], "w1v": f["nsa_cmp_w1_v"], "w2k": f["nsa_cmp_w2_k"], "w2v": f["nsa_cmp_w2_v"],
           "spread": np.repeat(np.eye(NACH, dtype=np.float32), DH, 1),
           "rpb": np.stack([f["rpb_2"][:, GR - 1 - r:2 * GR - 1 - r] for r in range(GR)]).reshape(GR, NH * GR, RB_C)}
    return {k: np.ascontiguousarray(v) for k, v in out.items()}


def kernel(**inputs):
    import concourse.bacc as bacc
    from concourse.bass_utils import run_bass_kernel_spmd

    nc = bacc.Bacc("TRN2", target_bir_lowering=False, num_devices=1)
    arrays, aps = {}, {}
    for name, a in lay_out(inputs).items():
        arrays[f"in_{name}"] = a
        aps[name] = nc.dram_tensor(f"in_{name}", a.shape, mybir.dt.from_np(a.dtype), kind="ExternalInput").ap()
    aps["out"] = nc.dram_tensor("out_x", (S, D), F32, kind="ExternalOutput").ap()
    two_blocks_kernel(nc, aps)
    r = run_bass_kernel_spmd(nc, [arrays], core_ids=[0])
    return np.asarray(r.results[0]["out_x"]).reshape(1, S, D)
```
